# Optimizing a Trainium2 kernel written in Bass

```python
import math
import jax, jax.numpy as jnp
from jax import lax
import numpy as np

D_MODEL = 1024
BATCH = 1
SEQ = 512
DEPTH = 2

HEAD_DIM = 64
A_Q_HEADS = 8
A_KV_HEADS = 2
WINDOW = 128
ROPE_DIM = HEAD_DIM // 4
ROPE_THETA = 500000.0
B_HEADS = 4
B_DK = 64
B_DV = 64
C_HEADS = 4
C_DK = 64
C_DV = 64
CONV_WIDTH = 4
CHUNK = 64
D_FF = -(-8 * D_MODEL // (3 * 256)) * 256
D_MIX = A_Q_HEADS * HEAD_DIM + B_HEADS * B_DV + C_HEADS * C_DV
C_CONV_CH = C_HEADS * (2 * C_DK + C_DV)
IN_SIZES = (A_Q_HEADS * HEAD_DIM, A_KV_HEADS * HEAD_DIM, A_KV_HEADS * HEAD_DIM,
            B_HEADS * B_DK, B_HEADS * B_DK, B_HEADS * B_DV, B_HEADS * B_DV,
            C_CONV_CH, C_HEADS * C_DV, C_HEADS, C_HEADS)
D_IN = sum(IN_SIZES)
NORM_EPS = 1e-6


def rmsnorm(x, gain):
    xf = x.astype(jnp.float32)
    y = xf * lax.rsqrt(jnp.mean(xf * xf, axis=-1, keepdims=True) + NORM_EPS)
    return (y * gain.astype(jnp.float32)).astype(x.dtype)

def l2norm(x):
    return x * lax.rsqrt(jnp.sum(x * x, axis=-1, keepdims=True) + NORM_EPS)

def partial_rope(x, positions):
    half = ROPE_DIM // 2
    inv_freq = ROPE_THETA ** (-jnp.arange(half, dtype=jnp.float32) * 2.0 / ROPE_DIM)
    ang = positions.astype(jnp.float32)[..., None] * inv_freq
    cos = jnp.cos(ang)[:, :, None, :]
    sin = jnp.sin(ang)[:, :, None, :]
    xf = x.astype(jnp.float32)
    x1, x2, xp = xf[..., :half], xf[..., half:ROPE_DIM], xf[..., ROPE_DIM:]
    out = jnp.concatenate([x1 * cos - x2 * sin, x2 * cos + x1 * sin, xp], axis=-1)
    return out.astype(x.dtype)

def sliding_window_attention(q, k, v, sinks):
    b, s, hq, d = q.shape
    hkv = k.shape[2]
    grp = hq // hkv
    nb = s // WINDOW
    qb = q.reshape(b, nb, WINDOW, hkv, grp, d)

    def band(t):
        tb = t.reshape(b, nb, WINDOW, hkv, d)
        prev = jnp.concatenate([jnp.zeros_like(tb[:, :1]), tb[:, :-1]], axis=1)
        return jnp.concatenate([prev, tb], axis=2)

    kb, vb = band(k), band(v)
    scores = jnp.einsum('bnqhgd,bnkhd->bnhgqk', qb, kb).astype(jnp.float32) * (d ** -0.5)
    qi = jnp.arange(WINDOW)[:, None]
    kj = jnp.arange(2 * WINDOW)[None, :]
    delta = qi + WINDOW - kj
    blk = jnp.arange(nb)[:, None, None]
    valid = (delta >= 0) & (delta < WINDOW) & (blk * WINDOW + kj - WINDOW >= 0)
    scores = jnp.where(valid[None, :, None, None], scores, -jnp.inf)
    sink = sinks.astype(jnp.float32).reshape(hkv, grp)[None, None, :, :, None, None]
    m = jnp.maximum(scores.max(axis=-1, keepdims=True), sink)
    p = jnp.exp(scores - m)
    denom = p.sum(axis=-1, keepdims=True) + jnp.exp(sink - m)
    out = jnp.einsum('bnhgqk,bnkhd->bnqhgd', (p / denom).astype(v.dtype), vb)
    return out.reshape(b, s, hq * d)

def hgrn2_chunked(q, log_f, v):
    b, s, h, dk = q.shape
    dv = v.shape[-1]
    nc = s // CHUNK

    def to_chunks(t):
        return t.reshape(b, nc, CHUNK, h, t.shape[-1]).transpose(1, 0, 3, 2, 4)

    causal = jnp.tril(jnp.ones((CHUNK, CHUNK), dtype=bool))

    def step(state, inp):
        qt, lf, vt = inp
        kt = -jnp.expm1(lf)
        cum = jnp.cumsum(lf, axis=2)
        diff = cum[:, :, :, None, :] - cum[:, :, None, :, :]
        decay = jnp.exp(jnp.where(causal[:, :, None], diff, -jnp.inf))
        attn = jnp.einsum('bhtd,bhsd,bhtsd->bhts', qt, kt, decay)
        o = attn @ vt + jnp.einsum('bhtd,bhde->bhte', qt * jnp.exp(cum), state)
        last = cum[:, :, -1:, :]
        state = jnp.exp(last[:, :, 0, :, None]) * state + jnp.einsum('bhsd,bhse->bhde', kt * jnp.exp(last - cum), vt)
        return state, o

    state0 = jnp.zeros((b, h, dk, dv), jnp.float32)
    _, o = lax.scan(step, state0, (to_chunks(q), to_chunks(log_f), to_chunks(v)))
    return o.transpose(1, 0, 3, 2, 4).reshape(b, s, h, dv)

def causal_depthwise_conv(x, w):
    ch = x.shape[-1]
    return lax.conv_general_dilated(x, w[:, None, :].astype(x.dtype), window_strides=(1,),
                                    padding=[(CONV_WIDTH - 1, 0)],
                                    dimension_numbers=('NWC', 'WIO', 'NWC'),
                                    feature_group_count=ch)

def gated_delta_chunked(q, k, v, beta, g):
    b, s, h, dk = q.shape
    dv = v.shape[-1]
    nc = s // CHUNK

    def to_chunks(t):
        return jnp.swapaxes(t.reshape((b, nc, CHUNK) + t.shape[2:]), 2, 3)

    qc, kc, vc, bc, gc = (to_chunks(t) for t in (q, k, v, beta, g))
    G = jnp.cumsum(gc, axis=-1)
    incl = jnp.tril(jnp.ones((CHUNK, CHUNK), dtype=bool))
    strict = jnp.tril(jnp.ones((CHUNK, CHUNK), dtype=bool), k=-1)
    L = jnp.exp(jnp.where(incl, G[..., :, None] - G[..., None, :], -jnp.inf))
    kb = kc * bc[..., None]
    A = jnp.where(strict, jnp.einsum('bnhtd,bnhsd->bnhts', kb, kc) * L, 0.0)
    eye = jnp.eye(CHUNK, dtype=jnp.float32)
    T = lax.linalg.triangular_solve(eye + A, jnp.broadcast_to(eye, A.shape), left_side=True,
                                    lower=True, unit_diagonal=True)
    U = T @ (vc * bc[..., None])
    W = T @ (kb * jnp.exp(G)[..., None])
    qk = jnp.where(incl, jnp.einsum('bnhtd,bnhsd->bnhts', qc, kc) * L, 0.0)
    q_dec = qc * jnp.exp(G)[..., None]
    k_dec = kc * jnp.exp(G[..., -1:] - G)[..., None]
    g_last = jnp.exp(G[..., -1])

    def step(state, inp):
        u, w, qd, kd, qkc, gl = inp
        v_new = u - w @ state
        o = qd @ state + qkc @ v_new
        state = gl[..., None, None] * state + jnp.swapaxes(kd, -1, -2) @ v_new
        return state, o

    xs = tuple(jnp.moveaxis(t, 1, 0) for t in (U, W, q_dec, k_dec, qk, g_last))
    state0 = jnp.zeros((b, h, dk, dv), jnp.float32)
    _, o = lax.scan(step, state0, xs)
    return jnp.swapaxes(jnp.moveaxis(o, 0, 1), 2, 3).reshape(b, s, h, dv)

def hybrid_mixer(h, positions, w_in, q_norm, k_norm, sinks, lb, hgrn_norm, conv_w, a_log, dt_bias,
                 gdn_norm, w_out):
    b, s, _ = h.shape
    f32 = jnp.float32
    proj = h @ w_in
    split_at = [int(i) for i in np.cumsum(IN_SIZES)[:-1]]
    aq, ak, av, bq, bf, bv, bg, cqkv, cg, cb, ca = jnp.split(proj, split_at, axis=-1)

    aq = partial_rope(rmsnorm(aq.reshape(b, s, A_Q_HEADS, HEAD_DIM), q_norm), positions)
    ak = partial_rope(rmsnorm(ak.reshape(b, s, A_KV_HEADS, HEAD_DIM), k_norm), positions)
    av = av.reshape(b, s, A_KV_HEADS, HEAD_DIM)
    out_a = sliding_window_attention(aq, ak, av, sinks)

    lb = lb.astype(f32).reshape(B_HEADS, B_DK)
    z = bf.reshape(b, s, B_HEADS, B_DK).astype(f32)
    log_f = jnp.logaddexp(jnp.log(lb), jnp.log1p(-lb) + jax.nn.log_sigmoid(z))
    o_b = hgrn2_chunked(bq.reshape(b, s, B_HEADS, B_DK).astype(f32), log_f,
                        bv.reshape(b, s, B_HEADS, B_DV).astype(f32))
    out_b = rmsnorm(o_b, hgrn_norm) * jax.nn.silu(bg.reshape(b, s, B_HEADS, B_DV).astype(f32))
    out_b = out_b.reshape(b, s, B_HEADS * B_DV).astype(h.dtype)

    cqkv = jax.nn.silu(causal_depthwise_conv(cqkv, conv_w))
    cq, ck, cv = jnp.split(cqkv, [C_HEADS * C_DK, 2 * C_HEADS * C_DK], axis=-1)
    cq = l2norm(cq.reshape(b, s, C_HEADS, C_DK).astype(f32)) * (C_DK ** -0.5)
    ck = l2norm(ck.reshape(b, s, C_HEADS, C_DK).astype(f32))
    cv = cv.reshape(b, s, C_HEADS, C_DV).astype(f32)
    beta = jax.nn.sigmoid(cb.astype(f32))
    g = -jnp.exp(a_log.astype(f32)) * jax.nn.softplus(ca.astype(f32) + dt_bias.astype(f32))
    o_c = gated_delta_chunked(cq, ck, cv, beta, g)
    out_c = rmsnorm(o_c, gdn_norm) * jax.nn.silu(cg.reshape(b, s, C_HEADS, C_DV).astype(f32))
    out_c = out_c.reshape(b, s, C_HEADS * C_DV).astype(h.dtype)

    mixed = jnp.concatenate([out_a, out_b, out_c], axis=-1)
    return mixed @ w_out

def swiglu(h, w_gate, w_up, w_down):
    return (jax.nn.silu(h @ w_gate) * (h @ w_up)) @ w_down

def first_inputs(seed: int = 0) -> dict:
    key = jax.random.key(seed)
    ks = jax.random.split(key, 24)
    f32 = jnp.float32

    def nrm(k, shape, scale):
        return jax.random.normal(k, shape, f32) * scale

    x = nrm(ks[0], (BATCH, SEQ, D_MODEL), 1.0)
    c = nrm(ks[1], (BATCH, D_MODEL), 1.0)
    positions = jnp.broadcast_to(jnp.arange(SEQ, dtype=jnp.int32)[None, :], (BATCH, SEQ))
    ada_w = nrm(ks[2], (DEPTH, D_MODEL, 6 * D_MODEL), 0.5 * D_MODEL ** -0.5)
    ada_b = nrm(ks[3], (DEPTH, 6 * D_MODEL), 0.02)
    norm_mix = 1.0 + nrm(ks[4], (DEPTH, D_MODEL), 0.05)
    w_in = nrm(ks[5], (DEPTH, D_MODEL, D_IN), D_MODEL ** -0.5)
    attn_q_norm = 1.0 + nrm(ks[6], (DEPTH, HEAD_DIM), 0.05)
    attn_k_norm = 1.0 + nrm(ks[7], (DEPTH, HEAD_DIM), 0.05)
    attn_sinks = nrm(ks[8], (DEPTH, A_Q_HEADS), 1.0)
    hgrn_lb_logits = nrm(ks[9], (DEPTH, B_HEADS * B_DK), 1.0)
    hgrn_out_norm = 1.0 + nrm(ks[10], (DEPTH, B_DV), 0.05)
    gdn_conv_w = nrm(ks[11], (DEPTH, CONV_WIDTH, C_CONV_CH), CONV_WIDTH ** -0.5)
    gdn_a_log = jnp.log(jax.random.uniform(ks[12], (DEPTH, C_HEADS), f32, 1.0, 16.0))
    dt = jnp.exp(jax.random.uniform(ks[13], (DEPTH, C_HEADS), f32, math.log(1e-3), math.log(1e-1)))
    gdn_dt_bias = dt + jnp.log(-jnp.expm1(-dt))
    gdn_out_norm = 1.0 + nrm(ks[14], (DEPTH, C_DV), 0.05)
    w_out = nrm(ks[15], (DEPTH, D_MIX, D_MODEL), D_MIX ** -0.5)
    norm_ffn = 1.0 + nrm(ks[16], (DEPTH, D_MODEL), 0.05)
    w_gate = nrm(ks[17], (DEPTH, D_MODEL, D_FF), D_MODEL ** -0.5)
    w_up = nrm(ks[18], (DEPTH, D_MODEL, D_FF), D_MODEL ** -0.5)
    w_down = nrm(ks[19], (DEPTH, D_FF, D_MODEL), D_FF ** -0.5)
    return {'x': x, 'c': c, 'positions': positions, 'ada_w': ada_w, 'ada_b': ada_b,
            'norm_mix': norm_mix, 'w_in': w_in, 'attn_q_norm': attn_q_norm,
            'attn_k_norm': attn_k_norm, 'attn_sinks': attn_sinks, 'hgrn_lb_logits': hgrn_lb_logits,
            'hgrn_out_norm': hgrn_out_norm, 'gdn_conv_w': gdn_conv_w, 'gdn_a_log': gdn_a_log,
            'gdn_dt_bias': gdn_dt_bias, 'gdn_out_norm': gdn_out_norm, 'w_out': w_out,
            'norm_ffn': norm_ffn, 'w_gate': w_gate, 'w_up': w_up, 'w_down': w_down}

def first_block(x, c, positions, ada_w, ada_b, norm_mix, w_in, attn_q_norm, attn_k_norm, attn_sinks,
              hgrn_lb_logits, hgrn_out_norm, gdn_conv_w, gdn_a_log, gdn_dt_bias, gdn_out_norm, w_out,
              norm_ffn, w_gate, w_up, w_down):
    lb_cum = jnp.cumsum(jax.nn.softmax(hgrn_lb_logits.astype(jnp.float32), axis=0), axis=0)
    lower_bounds = lb_cum - lb_cum[:1]
    cond = jax.nn.silu(c)
    for l in range(DEPTH):
        mod = cond @ ada_w[l] + ada_b[l]
        sh_m, sc_m, gt_m, sh_f, sc_f, gt_f = [m[:, None, :] for m in jnp.split(mod, 6, axis=-1)]
        h = rmsnorm(x, norm_mix[l]) * (1 + sc_m) + sh_m
        y = hybrid_mixer(h, positions, w_in[l], attn_q_norm[l], attn_k_norm[l], attn_sinks[l],
                         lower_bounds[l], hgrn_out_norm[l], gdn_conv_w[l], gdn_a_log[l],
                         gdn_dt_bias[l], gdn_out_norm[l], w_out[l])
        x = x + gt_m * y
        h = rmsnorm(x, norm_ffn[l]) * (1 + sc_f) + sh_f
        x = x + gt_f * swiglu(h, w_gate[l], w_up[l], w_down[l])
    return x


GRID_W = 64
CTX_LEN = 256
A_HEADS = 8
A_HEAD_DIM = 64
ROPE_THETA_2 = 10000.0
Q_BLOCK = 128
B_HEAD_DIM = 128
B_CHUNK = 128
B_CONV = 3
POOL_WINDOWS = (2, 4, 8, 16)
POOL_GROUP = D_MODEL // 4
N_EXPERTS = 16
EC_FACTOR = 2
D_EXPERT = 1024

A_Q = A_HEADS * A_HEAD_DIM
A_KV = A_KV_HEADS * A_HEAD_DIM
B_W = B_HEADS * B_HEAD_DIM
N_GATES = 2 * 2 * B_HEADS
EVEN_IN = A_Q + 2 * A_KV + 4 * B_W + N_GATES
MIX_W = A_Q + B_W
EVEN_SPLITS = (A_Q, A_Q + A_KV, A_Q + 2 * A_KV, A_Q + 2 * A_KV + B_W, A_Q + 2 * A_KV + 2 * B_W,
               A_Q + 2 * A_KV + 3 * B_W, A_Q + 2 * A_KV + 4 * B_W)
N_EVEN = (DEPTH + 1) // 2
N_ODD = DEPTH // 2


def rmsnorm_2(x, g):
    xf = x.astype(jnp.float32)
    y = xf * lax.rsqrt(jnp.mean(xf * xf, axis=-1, keepdims=True) + NORM_EPS)
    return (y * g.astype(jnp.float32)).astype(x.dtype)

def adaln(cond, w, b):
    m = jax.nn.silu(cond) @ w + b
    return m.reshape(cond.shape[:-1] + (1, 6, D_MODEL))

def modulate(x, g, shift, scale):
    return rmsnorm_2(x, g) * (1 + scale) + shift

def axial_rope(n_tokens):
    rows = n_tokens // GRID_W
    row_ids = jnp.repeat(jnp.arange(rows, dtype=jnp.float32), GRID_W)
    col_ids = jnp.tile(jnp.arange(GRID_W, dtype=jnp.float32), rows)
    half = A_HEAD_DIM // 2
    inv = ROPE_THETA_2 ** (-jnp.arange(0, half, 2, dtype=jnp.float32) / half)
    ang = jnp.stack([row_ids[:, None] * inv, col_ids[:, None] * inv], axis=1)
    return jnp.cos(ang), jnp.sin(ang)

def apply_rope(x, cos, sin):
    Bn, n, H, d = x.shape
    xr = x.reshape(Bn, n, H, 2, 2, d // 4)
    x1, x2 = xr[..., 0, :], xr[..., 1, :]
    c = cos[None, :, None].astype(x.dtype)
    s = sin[None, :, None].astype(x.dtype)
    return jnp.stack([x1 * c - x2 * s, x2 * c + x1 * s], axis=-2).reshape(x.shape)

def attend_blocks(q, k, v):
    Bn, Lq, _, d = q.shape
    G = A_HEADS // A_KV_HEADS
    nb = Lq // Q_BLOCK
    qb = q.reshape(Bn, nb, Q_BLOCK, A_KV_HEADS, G, d).transpose(1, 0, 3, 4, 2, 5)
    kt = jnp.swapaxes(k, 1, 2)
    vt = jnp.swapaxes(v, 1, 2)
    scale = d ** -0.5

    def one_block(qblk):
        s = jnp.einsum('bhgtd,bhsd->bhgts', qblk, kt).astype(jnp.float32) * scale
        p = jax.nn.softmax(s, axis=-1).astype(vt.dtype)
        return jnp.einsum('bhgts,bhsd->bhgtd', p, vt)

    o = lax.map(one_block, qb)
    return o.transpose(1, 0, 4, 2, 3, 5).reshape(Bn, Lq, A_HEADS * d)

def short_conv(x, w):
    n = x.shape[1]
    pad = B_CONV // 2
    xp = jnp.pad(x, ((0, 0), (pad, B_CONV - 1 - pad), (0, 0)))
    return sum(xp[:, j:j + n] * w[j] for j in range(B_CONV))

def mlstm_zero_state(Bn):
    return (jnp.zeros((Bn, B_HEADS, B_HEAD_DIM, B_HEAD_DIM), jnp.float32),
            jnp.zeros((Bn, B_HEADS, B_HEAD_DIM), jnp.float32),
            jnp.full((Bn, B_HEADS), -1e30, jnp.float32))

def mlstm_scan(q, k, v, ig, lf, state):
    Bn, H, L, d = q.shape
    nc = L // B_CHUNK
    k = k * (d ** -0.5)

    def to_chunks(a):
        a = a.reshape(a.shape[:2] + (nc, B_CHUNK) + a.shape[3:])
        return jnp.moveaxis(a, 2, 0)

    tril = jnp.tril(jnp.ones((B_CHUNK, B_CHUNK), dtype=bool))

    def step(carry, inp):
        C, n, m = carry
        qc, kc, vc, ic, fc = inp
        b = jnp.cumsum(fc, axis=-1)
        log_d = jnp.where(tril, b[..., :, None] - b[..., None, :] + ic[..., None, :], -jnp.inf)
        log_inter = m[..., None] + b
        m_t = jnp.maximum(log_inter, jnp.max(log_d, axis=-1))
        w_intra = jnp.exp(log_d - m_t[..., None]) * jnp.einsum('bhtd,bhsd->bhts', qc, kc)
        w_inter = jnp.exp(log_inter - m_t)
        num = (w_inter[..., None] * jnp.einsum('bhed,bhtd->bhte', C, qc)
               + jnp.einsum('bhts,bhse->bhte', w_intra, vc))
        den = w_inter * jnp.einsum('bhd,bhtd->bht', n, qc) + jnp.sum(w_intra, axis=-1)
        h = num / jnp.maximum(jnp.abs(den), jnp.exp(-m_t))[..., None]
        b_end = b[..., -1]
        log_w = b_end[..., None] - b + ic
        m_new = jnp.maximum(m + b_end, jnp.max(log_w, axis=-1))
        w_s = jnp.exp(log_w - m_new[..., None])
        decay = jnp.exp(m + b_end - m_new)
        C = decay[..., None, None] * C + jnp.einsum('bhs,bhse,bhsd->bhed', w_s, vc, kc)
        n = decay[..., None] * n + jnp.einsum('bhs,bhsd->bhd', w_s, kc)
        return (C, n, m_new), h

    state, h = lax.scan(step, state, tuple(to_chunks(a) for a in (q, k, v, ig, lf)))
    h = jnp.moveaxis(h, 0, 2).reshape(Bn, H, L, d)
    return h, state

def mlstm_bidir(q, k, v, ig, lf, states):
    h_f, s_f = mlstm_scan(q, k, v, ig[0], lf[0], states[0])
    flip = lambda a: jnp.flip(a, axis=2)
    h_b, s_b = mlstm_scan(flip(q), flip(k), flip(v), flip(ig[1]), flip(lf[1]), states[1])
    return h_f + flip(h_b), (s_f, s_b)

def even_mixer(h_lat, h_ctx, ctx_out, w_in, w_out, g_qn, g_kn, w_conv, b_gate, g_hn):
    Bn, L, _ = h_lat.shape

    def project(h):
        n = h.shape[1]
        qa, ka, va, qb, kb, vb, ob, gt = jnp.split(h @ w_in, EVEN_SPLITS, axis=-1)
        qa = rmsnorm_2(qa.reshape(Bn, n, A_HEADS, A_HEAD_DIM), g_qn)
        ka = rmsnorm_2(ka.reshape(Bn, n, A_KV_HEADS, A_HEAD_DIM), g_kn)
        va = va.reshape(Bn, n, A_KV_HEADS, A_HEAD_DIM)
        qk = jax.nn.silu(short_conv(jnp.concatenate([qb, kb], axis=-1), w_conv))
        to_heads = lambda a: a.reshape(Bn, n, B_HEADS, B_HEAD_DIM).transpose(0, 2, 1, 3).astype(jnp.float32)
        qm, km, vm = to_heads(qk[..., :B_W]), to_heads(qk[..., B_W:]), to_heads(vb)
        g = (gt + b_gate).astype(jnp.float32).reshape(Bn, n, 2, 2, B_HEADS).transpose(2, 3, 0, 4, 1)
        ig = g[:, 0]
        lf = jax.nn.log_sigmoid(g[:, 1])
        return (qa, ka, va), (qm, km, vm, ig, lf), ob

    def mlstm_out(hm, ob):
        n = hm.shape[2]
        hm = rmsnorm_2(jnp.swapaxes(hm, 1, 2), g_hn.reshape(B_HEADS, B_HEAD_DIM))
        return hm.reshape(Bn, n, B_W).astype(ob.dtype) * jax.nn.sigmoid(ob)

    (qa_c, ka_c, va_c), mc, ob_c = project(h_ctx)
    (qa_l, ka_l, va_l), ml, ob_l = project(h_lat)
    cos, sin = axial_rope(L)
    qa_l = apply_rope(qa_l, cos, sin)
    ka_l = apply_rope(ka_l, cos, sin)
    o_a = attend_blocks(qa_l, jnp.concatenate([ka_c, ka_l], axis=1), jnp.concatenate([va_c, va_l], axis=1))
    st0 = mlstm_zero_state(Bn)
    h_c, ctx_states = mlstm_bidir(*mc, (st0, st0))
    h_l, _ = mlstm_bidir(*ml, ctx_states)
    y = jnp.concatenate([o_a, mlstm_out(h_l, ob_l)], axis=-1) @ w_out
    yc = None
    if ctx_out:
        yc = jnp.concatenate([attend_blocks(qa_c, ka_c, va_c), mlstm_out(h_c, ob_c)], axis=-1) @ w_out
    return y, yc

def pool_mixer(h, w_in, w_grp, s_pool):
    Bn, n, _ = h.shape
    u = h @ w_in
    uf = u.astype(jnp.float32)
    S = jnp.pad(jnp.cumsum(uf, axis=1), ((0, 0), (1, 0), (0, 0)))
    t = jnp.arange(n)
    outs = []
    for gi, w in enumerate(POOL_WINDOWS):
        lo = w // 2
        hi = w - 1 - lo
        a = jnp.clip(t - lo, 0, n - 1)
        e = jnp.clip(t + hi, 0, n - 1)
        Sg = S[:, :, gi * POOL_GROUP:(gi + 1) * POOL_GROUP]
        cnt = (e - a + 1).astype(jnp.float32)[None, :, None]
        outs.append((Sg[:, e + 1] - Sg[:, a]) / cnt - uf[:, :, gi * POOL_GROUP:(gi + 1) * POOL_GROUP])
    p = jnp.stack(outs, axis=2).astype(u.dtype)
    y = jnp.einsum('bngc,gce->bnge', p, w_grp).reshape(Bn, n, D_MODEL)
    return y * s_pool

def ec_moe(h, w_router, w_gate, w_up, w_down):
    Bn, n, Dm = h.shape
    cap = max(1, EC_FACTOR * n // N_EXPERTS)
    aff = jax.nn.softmax(jnp.einsum('bnd,de->bne', h, w_router).astype(jnp.float32), axis=-1)
    gate, idx = lax.top_k(jnp.swapaxes(aff, 1, 2), cap)
    xs = jax.vmap(lambda hb, ib: hb[ib])(h, idx)
    a = jax.nn.silu(jnp.einsum('becd,edf->becf', xs, w_gate)) * jnp.einsum('becd,edf->becf', xs, w_up)
    out = jnp.einsum('becf,efd->becd', a, w_down) * gate[..., None].astype(h.dtype)
    return jax.vmap(lambda ob, ib: jnp.zeros((n, Dm), ob.dtype).at[ib.reshape(-1)].add(ob.reshape(-1, Dm)))(out, idx)

def second_inputs(seed: int = 0) -> dict:
    key = jax.random.key(seed)
    ks = jax.random.split(key, 23)
    nrm = lambda k, shape, s: s * jax.random.normal(k, shape, jnp.float32)
    fb = jnp.linspace(3.0, 6.0, B_HEADS)
    gate_base = jnp.concatenate([jnp.zeros((B_HEADS,)), fb, jnp.zeros((B_HEADS,)), fb])
    return {
        "x": nrm(ks[0], (BATCH, SEQ, D_MODEL), 1.0),
        "c": nrm(ks[1], (BATCH, D_MODEL), 1.0),
        "ctx": nrm(ks[2], (BATCH, CTX_LEN, D_MODEL), 1.0),
        "c_ctx": nrm(ks[3], (D_MODEL,), 1.0),
        "w_mod": nrm(ks[4], (DEPTH, D_MODEL, 6 * D_MODEL), 0.5 * D_MODEL ** -0.5),
        "b_mod": nrm(ks[5], (DEPTH, 6 * D_MODEL), 0.02),
        "g_norm1": 1.0 + nrm(ks[6], (DEPTH, D_MODEL), 0.02),
        "g_norm2": 1.0 + nrm(ks[7], (DEPTH, D_MODEL), 0.02),
        "w_in_even": nrm(ks[8], (N_EVEN, D_MODEL, EVEN_IN), D_MODEL ** -0.5),
        "w_out_even": nrm(ks[9], (N_EVEN, MIX_W, D_MODEL), MIX_W ** -0.5),
        "g_qnorm": 1.0 + nrm(ks[10], (N_EVEN, A_HEAD_DIM), 0.02),
        "g_knorm": 1.0 + nrm(ks[11], (N_EVEN, A_HEAD_DIM), 0.02),
        "w_conv": nrm(ks[12], (N_EVEN, B_CONV, 2 * B_W), B_CONV ** -0.5),
        "b_gate": gate_base[None] + nrm(ks[13], (N_EVEN, N_GATES), 0.1),
        "g_hnorm": 1.0 + nrm(ks[14], (N_EVEN, B_W), 0.02),
        "w_in_odd": nrm(ks[15], (N_ODD, D_MODEL, D_MODEL), D_MODEL ** -0.5),
        "w_pool_grp": nrm(ks[16], (N_ODD, 4, POOL_GROUP, POOL_GROUP), POOL_GROUP ** -0.5),
        "s_pool": 1.0 + nrm(ks[17], (N_ODD, D_MODEL), 0.1),
        "w_router": nrm(ks[18], (DEPTH, D_MODEL, N_EXPERTS), D_MODEL ** -0.5),
        "w_exp_gate": nrm(ks[19], (DEPTH, N_EXPERTS, D_MODEL, D_EXPERT), D_MODEL ** -0.5),
        "w_exp_up": nrm(ks[20], (DEPTH, N_EXPERTS, D_MODEL, D_EXPERT), D_MODEL ** -0.5),
        "w_exp_down": nrm(ks[21], (DEPTH, N_EXPERTS, D_EXPERT, D_MODEL), D_EXPERT ** -0.5),
        "g_final": 1.0 + nrm(ks[22], (D_MODEL,), 0.02),
    }

def second_block(x, c, ctx, c_ctx, w_mod, b_mod, g_norm1, g_norm2, w_in_even, w_out_even, g_qnorm, g_knorm,
              w_conv, b_gate, g_hnorm, w_in_odd, w_pool_grp, s_pool, w_router, w_exp_gate, w_exp_up,
              w_exp_down, g_final):
    xc = ctx
    for i in range(DEPTH):
        ctx_next = any(j % 2 == 0 for j in range(i + 1, DEPTH))
        ctx_used = (i % 2 == 0) or ctx_next
        m_lat = adaln(c, w_mod[i], b_mod[i])
        h = modulate(x, g_norm1[i], m_lat[..., 0, :], m_lat[..., 1, :])
        yc = None
        if ctx_used:
            m_ctx = adaln(c_ctx, w_mod[i], b_mod[i])
            hc = modulate(xc, g_norm1[i], m_ctx[..., 0, :], m_ctx[..., 1, :])
        if i % 2 == 0:
            e = i // 2
            y, yc = even_mixer(h, hc, ctx_next, w_in_even[e], w_out_even[e], g_qnorm[e], g_knorm[e],
                               w_conv[e], b_gate[e], g_hnorm[e])
        else:
            o = i // 2
            y = pool_mixer(h, w_in_odd[o], w_pool_grp[o], s_pool[o])
            if ctx_next:
                yc = pool_mixer(hc, w_in_odd[o], w_pool_grp[o], s_pool[o])
        x = x + m_lat[..., 2, :] * y
        h = modulate(x, g_norm2[i], m_lat[..., 3, :], m_lat[..., 4, :])
        x = x + m_lat[..., 5, :] * ec_moe(h, w_router[i], w_exp_gate[i], w_exp_up[i], w_exp_down[i])
        if ctx_next:
            xc = xc + m_ctx[..., 2, :] * yc
            hc = modulate(xc, g_norm2[i], m_ctx[..., 3, :], m_ctx[..., 4, :])
            xc = xc + m_ctx[..., 5, :] * ec_moe(hc, w_router[i], w_exp_gate[i], w_exp_up[i], w_exp_down[i])
    return rmsnorm_2(x, g_final)


def setup_inputs(seed=0):
    out = dict(first_inputs(seed))
    for name, value in second_inputs(seed + 1).items():
        if name != "x":
            out[name + "_2"] = value
    return out


def reference(
    x, c, positions, ada_w, ada_b, norm_mix, w_in, attn_q_norm, attn_k_norm, attn_sinks,
    hgrn_lb_logits, hgrn_out_norm, gdn_conv_w, gdn_a_log, gdn_dt_bias, gdn_out_norm, w_out,
    norm_ffn, w_gate, w_up, w_down, c_2, ctx_2, c_ctx_2, w_mod_2, b_mod_2, g_norm1_2, g_norm2_2,
    w_in_even_2, w_out_even_2, g_qnorm_2, g_knorm_2, w_conv_2, b_gate_2, g_hnorm_2, w_in_odd_2,
    w_pool_grp_2, s_pool_2, w_router_2, w_exp_gate_2, w_exp_up_2, w_exp_down_2, g_final_2,
):
    x = first_block(
        x, c, positions, ada_w, ada_b, norm_mix, w_in, attn_q_norm, attn_k_norm, attn_sinks,
        hgrn_lb_logits, hgrn_out_norm, gdn_conv_w, gdn_a_log, gdn_dt_bias, gdn_out_norm, w_out,
        norm_ffn, w_gate, w_up, w_down,
    )
    return second_block(
        x, c_2, ctx_2, c_ctx_2, w_mod_2, b_mod_2, g_norm1_2, g_norm2_2, w_in_even_2,
        w_out_even_2, g_qnorm_2, g_knorm_2, w_conv_2, b_gate_2, g_hnorm_2, w_in_odd_2,
        w_pool_grp_2, s_pool_2, w_router_2, w_exp_gate_2, w_exp_up_2, w_exp_down_2, g_final_2,
    )


_drawn_inputs = setup_inputs


def setup_inputs(seed=0):
    import zlib

    import numpy as np

    out = dict(_drawn_inputs(seed))
    spreads = {}
    factors = {'attn_q_norm': 8.0,
     'attn_k_norm': 8.0,
     'attn_sinks': 8.0,
     'hgrn_out_norm': 5.556,
     'gdn_out_norm': 7.043,
     'ctx_2': 3.091,
     'g_norm1_2': 8.0,
     'g_norm2_2': 6.673,
     'g_qnorm_2': 8.0,
     'g_knorm_2': 8.0,
     'g_hnorm_2': 8.0,
     'g_final_2': 2.965}
    for name, (base, spread) in spreads.items():
        noise = np.random.default_rng([zlib.crc32(name.encode()), seed]).standard_normal(out[name].shape)
        drawn = base * np.exp(spread * noise) if base else spread * noise
        out[name] = __import__('jax').numpy.asarray(drawn.astype(out[name].dtype))
    for name, factor in factors.items():
        out[name] = (out[name] * factor).astype(out[name].dtype)
    return out
```

```python
from contextlib import ExitStack

import numpy as np

import concourse.bass as bass
from concourse import mybir

ALU = mybir.AluOpType
ACT = mybir.ActivationFunctionType
F32 = mybir.dt.float32
I32 = mybir.dt.int32
F32R = mybir.dt.float32r
AX = mybir.AxisListType

P = 128
D = 1024
KB = D // P
T = 512
NT = T // P
TC = 256
NC = TC // P
FF = 2816
FB = FF // P
E = 16
CAP = 2 * T // E
EPS = 1e-6
RING = 8
PANEL = 2048
H1 = 4
LEVELS = (64, 32, 16, 8, 4, 2, 1)
NEG = -1e30
POOLS = (2, 4, 8, 16)
CTX_BLOCKS = (4, 5, 10, 11, 12, 13, 14, 15, 16, 17, 22)
M_BACK = (1, 0, 5, 4, 3, 2)
PAD = 8



def constants():
    i = np.arange(P)
    row, col = i[:, None], i[None, :]
    c = {}
    c["ident"] = row == col
    c["ones"] = np.ones((P, P))
    c["halves"] = row // 64 == col // 64
    for g in range(2):
        c[f"dup{g}"] = row == g * 64 + col % 64
    c["upto"] = row <= col
    c["below"] = row < col
    c["from"] = row >= col
    rope = np.zeros((P, P))
    axial = np.zeros((P, P))
    for m in range(P):
        base, d = m // 64 * 64, m % 64
        if d < 8:
            rope[base + d + 8, m] = -1
        elif d < 16:
            rope[base + d - 8, m] = 1
        if d % 32 < 16:
            axial[m + 16, m] = -1
        else:
            axial[m - 16, m] = 1
    c["rot_rope"] = rope
    c["rot_axial"] = axial
    c["iota"] = np.broadcast_to(np.arange(CAP)[None, :], (P, CAP))
    d = i % 64
    half = 8
    freq = np.zeros(P)
    inv = (np.float32(500000.0) ** (-np.arange(half, dtype=np.float32) * np.float32(2.0) / np.float32(16))).astype(np.float32)
    freq[d < 16] = inv[d[d < 16] % 8]
    c["freq"] = freq[:, None]
    first = {}
    for s in LEVELS:
        first[f"level{s}"] = (row // (2 * s) == col // (2 * s)) & (row % (2 * s) < s) & (col % (2 * s) >= s)
    first["resets"] = np.broadcast_to((np.arange(T) % P != 0)[None, :], (P, T))
    kj = np.arange(2 * P)[None, :]
    delta = row + P - kj
    ok = (delta >= 0) & (delta < P)
    first["band"] = np.where(ok, 0.0, NEG)
    first["band0"] = np.where(ok & (kj >= P), 0.0, NEG)
    even = {}
    t = np.arange(T)
    finv = (np.float32(10000.0) ** (-np.arange(0, 32, 2, dtype=np.float32) / np.float32(32))).astype(np.float32)
    where = np.where((d < 32)[:, None], (t // 64)[None, :], (t % 64)[None, :]).astype(np.float32)
    ang = where * finv[d % 16][:, None]
    even["cos"], even["sin"] = np.cos(ang), np.sin(ang)
    even["mask_f"] = np.where(row >= col, 0.0, NEG)
    even["mask_b"] = np.where(row <= col, 0.0, NEG)
    pool = {}
    for w in POOLS:
        lo, hi = w // 2, w - 1 - w // 2
        n = np.clip(t + hi, 0, T - 1) - np.clip(t - lo, 0, T - 1) + 1
        pool[f"count{w}"] = np.broadcast_to((1.0 / n)[None, :], (P, T))
    return c, first, even, pool


def packed(tables):
    at, n = {}, 0
    for name, a in tables.items():
        at[name] = (n, n + a.shape[1])
        n += a.shape[1]
    return np.ascontiguousarray(np.concatenate([np.asarray(a, np.float32) for a in tables.values()], 1)), at



def columns(v):
    return np.asarray(v).reshape(-1, P).T


def twice(v):
    return np.concatenate([np.asarray(v)] * 2)[:, None]


def rows(v):
    return np.broadcast_to(np.asarray(v)[None, :], (P, len(v)))


def parameters(a):
    t = {}
    for l in range(2):
        t[f"norm_mix{l}"] = columns(a["norm_mix"][l])
        t[f"norm_ffn{l}"] = columns(a["norm_ffn"][l])
        t[f"ada_b{l}"] = columns(a["ada_b"][l])
        t[f"q_norm{l}"] = twice(a["attn_q_norm"][l])
        t[f"k_norm{l}"] = twice(a["attn_k_norm"][l])
        t[f"hgrn_norm{l}"] = twice(a["hgrn_out_norm"][l])
        t[f"gdn_norm{l}"] = twice(a["gdn_out_norm"][l])
        t[f"conv{l}"] = np.concatenate([columns(w) for w in a["gdn_conv_w"][l]], 1)
        t[f"sinks{l}"] = rows(a["attn_sinks"][l])
        t[f"a_log{l}"] = rows(a["gdn_a_log"][l])
        t[f"dt{l}"] = rows(a["gdn_dt_bias"][l])
        t[f"lb{l}"] = columns(a["hgrn_lb_logits"][l])
        t[f"b_mod{l}"] = columns(a["b_mod_2"][l])
        t[f"norm1{l}"] = columns(a["g_norm1_2"][l])
        t[f"norm2{l}"] = columns(a["g_norm2_2"][l])
        t[f"router{l}"] = np.asarray(a["w_router_2"][l]).reshape(KB, P, E).transpose(1, 0, 2).reshape(P, KB * E)
    t["c"] = columns(a["c"][0])
    t["c2"] = columns(a["c_2"][0])
    t["c_ctx"] = columns(a["c_ctx_2"])
    t["gq"] = twice(a["g_qnorm_2"][0])
    t["gk"] = twice(a["g_knorm_2"][0])
    t["conv_e"] = np.concatenate([columns(w) for w in a["w_conv_2"][0]], 1)
    t["b_gate"] = rows(a["b_gate_2"][0])
    t["hnorm"] = columns(a["g_hnorm_2"][0])
    t["s_pool"] = columns(a["s_pool_2"][0])
    t["final"] = columns(a["g_final_2"])
    return t


class Vector:

    def __init__(self, weights, layer, v, cond, to):
        self.weights, self.layer, self.v, self.cond, self.to = weights, layer, v, cond, to
        self.bias = f"ada_b{layer}" if weights == "ada_w" else f"b_mod{layer}"


PLANS = {
    "start": [Vector("ada_w", 0, v, 0, (0,)) for v in (0, 1)],
    "layer0": [Vector("ada_w", 0, v, 0, (0,)) for v in (2, 3, 4, 5)] + [Vector("ada_w", 1, v, 0, (0,)) for v in (0, 1)],
    "layer1": [Vector("ada_w", 1, v, 0, (0,)) for v in (2, 3, 4, 5)] + [Vector("w_mod", 0, v, 1, (0, 1)) for v in (0, 1)],
    "even": [Vector("w_mod", 0, v, 0, (0,)) for v in (2, 3, 4, 5)] + [Vector("w_mod", 1, v, 0, (1,)) for v in range(6)],
}
CONDITIONS = {"start": (("c",),), "layer0": (("c",),), "layer1": (("c",), ("c2", "c_ctx")), "even": (("c2",),)}


class Due:

    def __init__(self, sem):
        self.sem, self.n = sem, {}

    def __call__(self, name, steps=1):
        key = TAKES.get(name, name)
        self.n[key] = self.n.get(key, 0) + steps
        return self.sem[name], self.n[key]


SIGNALS = {
    "x_in": "DMA: x has landed", "const_in": "DMA: constants, parameters, tables, positions",
    "pos_in": "DMA: the positions again", "stored": "DMA: the output is in DRAM",
    "stage": "an engine is through with a stage",
    "act_step": "ScalarE: its last linked instruction is done", "dve_step": "VectorE: its last linked instruction is done",
    "panel_used": "TensorE: a panel of the ring is free",
    "lb": "VectorE: difference of the bounds' logits", "lb_exp": "ScalarE: its exponential",
    "cond_exp": "ScalarE: exp(-c)", "cond": "VectorE: silu(c), repeated",
    "mod_row": "TensorE: a modulation vector as four rows", "mod_sb": "ScalarE: those rows in SBUF",
    "mod_tr": "TensorE: the rows turned to columns", "mod_ready": "VectorE: a modulation vector as columns",
    "half_used": "TensorE: the upper halves of a panel may be replaced", "hi": "ScalarE: the upper halves of a panel or block", "lo": "VectorE: its lower halves",
    "sq": "ScalarE: squares of a block", "sq_sum": "TensorE: the sums of squares so far",
    "rstd": "ScalarE: reciprocal root of the mean square", "xn": "VectorE: a normalised block",
    "h": "ScalarE: a block of the modulated norm", "lin": "TensorE: a block of a projection",
    "proj": "ScalarE: that block in SBUF", "y": "TensorE: a block of the mixer's output", "y_used": "VectorE: added to x",
    "gn_sq": "ScalarE: squares", "gn_sum": "TensorE: their sums over a head", "gn_rstd": "ScalarE: reciprocal root",
    "gn": "VectorE: a block normalised by head", "trig": "VectorE: angles", "trig_sb": "ScalarE: their sines",
    "rot": "TensorE: the rotated halves", "roped": "VectorE: a block with rope",
    "krep_pad": "VectorE: zeros before the first key",
    "krep": "TensorE: a k head in both halves", "krep_sb": "ScalarE: in SBUF",
    "vt": "TensorE: v by tokens", "vt_sb": "ScalarE: in SBUF",
    "score": "TensorE: a head's scores", "smax": "VectorE: masked, and their maxima", "pexp": "ScalarE: exponentials",
    "w_mixed": "VectorE: a head's output by tokens, normalised", "probT": "TensorE: turned", "probT_sb": "ScalarE: in SBUF",
    "att": "TensorE: a head's output", "mixed": "ScalarE: in SBUF",
    "gate_exp": "ScalarE: exp(-gate)",
    "b_z": "VectorE: clamped logits", "b_ez": "ScalarE: exp(-z)", "b_f": "VectorE: forget gates", "b_lf": "ScalarE: their logs",
    "b_qk": "VectorE: a level's q and k", "b_score": "TensorE: a head's scores", "b_acc": "VectorE: taken where they hold",
    "b_diff": "VectorE: distance to the level's middle", "b_decay": "ScalarE: its decay", "b_qd": "VectorE: distance to the chunk's end",
    "b_v": "TensorE: v by tokens", "b_v_sb": "ScalarE: in SBUF", "b_kd": "VectorE: decayed q and k",
    "b_kdT": "TensorE: k by tokens", "b_kdT_sb": "ScalarE: in SBUF", "b_state": "VectorE: the state before a chunk",
    "b_ds": "TensorE: what a chunk adds", "b_out": "TensorE: the output",
    "conv": "VectorE: a convolved block", "conv_exp": "ScalarE: exp(-x)", "conv_done": "VectorE: its silu",
    "g_gates": "TensorE: the gates by tokens", "g_gates_sb": "ScalarE: in SBUF, exp(-b), exp(a_log)",
    "g_v": "TensorE: v by tokens", "g_v_raw": "ScalarE: in SBUF", "g_sum": "VectorE: a + dt", "g_ln": "ScalarE: log(1 + exp(-|a|))",
    "g_g": "VectorE: log decays", "g_cum": "TensorE: their sums", "g_cols": "ScalarE: in SBUF",
    "g_rows": "TensorE: a head's sums along the free dimension", "g_eg": "ScalarE: their exponentials",
    "g_diffs": "VectorE: their differences", "g_diff": "VectorE: clamped", "g_decay": "ScalarE: decays",
    "g_kdiff": "VectorE: distance to the chunk's end", "g_kdf": "ScalarE: its decay", "g_brows": "TensorE: a head's beta rows",
    "g_kb": "VectorE: k beta", "g_k": "TensorE: k by tokens", "g_k_sb": "ScalarE: in SBUF",
    "g_score": "TensorE: a head's products", "g_acc": "VectorE: with decay", "g_y": "VectorE: the first level's inverse",
    "g_t": "TensorE: it, turned", "g_t_sb": "ScalarE: in SBUF", "g_al": "VectorE: a level's blocks of two heads",
    "g_x": "TensorE: A T", "g_x_sb": "ScalarE: in SBUF", "g_dy": "TensorE: X^T Y", "g_dt": "TensorE: T X",
    "g_yt": "VectorE: Y of a level", "g_tt": "VectorE: T of a level",
    "g_state": "VectorE: the state before a chunk", "w_att": "TensorE: a head's output by tokens", "recip": "VectorE: reciprocal sums", "g_r": "TensorE: k S", "g_rhs": "VectorE: v - k S",
    "g_vn": "TensorE: T (v - k S)", "g_vn_sb": "ScalarE: in SBUF", "g_ds": "TensorE: the output, and what a chunk adds",
    "gu": "TensorE: a block of gate, then of up", "ff_exp": "ScalarE: exp(-gate)", "ff": "VectorE: silu(gate) up",
    "down": "TensorE: a block of the output", "down_x": "VectorE: added to x",
    "ctx_in": "DMA: the context and the layer's tables", "pool_in": "DMA: the pooling tables",
    "lin_c": "TensorE: a block of the context's projection", "proj_c": "ScalarE: in SBUF",
    "m_gates": "TensorE: gates by tokens", "m_raw": "ScalarE: in SBUF", "m_tok": "TensorE: a tile of v or k by tokens",
    "m_tok_sb": "ScalarE: in SBUF", "m_sp": "VectorE: gates with bias", "m_ln": "ScalarE: log(1 + exp(-|f|))",
    "m_lf": "VectorE: log forget gates", "m_b": "TensorE: their sums", "m_b_sb": "ScalarE: in SBUF",
    "m_a": "VectorE: input gates less the sums", "m_rows": "TensorE: a step's row of them, on all partitions",
    "m_cols": "VectorE: a step's exponents", "m_ws": "ScalarE: weights of keys and of the state",
    "m_log": "VectorE: log weights", "m_exp": "ScalarE: weights", "m_qk": "TensorE: q k", "m_w": "VectorE: weighted scores",
    "m_wT": "TensorE: turned", "m_wT_sb": "ScalarE: in SBUF", "m_inter": "TensorE: q against the state",
    "m_num": "TensorE: scores against v", "m_kw": "VectorE: weighted keys", "m_ds": "TensorE: what a step adds",
    "m_state": "VectorE: the state after a step", "m_ss": "VectorE: sums of squares", "m_rs": "ScalarE: reciprocal roots",
    "m_h": "VectorE: normalised output", "m_hT": "TensorE: a head of it by features",
    "r_logits": "TensorE: router logits", "r_sub": "VectorE: less their maxima", "r_exp": "ScalarE: exponentials",
    "r_tok": "TensorE: h by tokens, half a tile", "r_tok_sb": "ScalarE: in SBUF", "r_aff": "VectorE: affinities",
    "r_affT": "TensorE: turned", "r_affT_sb": "ScalarE: in SBUF", "r_thr": "VectorE: each expert's 64th largest",
    "r_thr_rows": "TensorE: on all partitions", "r_thr_sb": "ScalarE: in SBUF", "r_marks": "VectorE: marks to be counted",
    "r_count": "TensorE: their running counts", "r_pg": "VectorE: a tile's gates by slot", "r_pgT": "TensorE: turned",
    "r_pgT_sb": "ScalarE: in SBUF", "x_sel": "TensorE: a pair's tokens", "x_sel_sb": "ScalarE: in SBUF",
    "e_gate": "TensorE: a pair's gates", "e_up": "TensorE: its ups", "e_exp": "ScalarE: exp(-gate)",
    "e_act": "VectorE: silu(gate) up", "aT": "TensorE: turned", "aT_sb": "ScalarE: in SBUF",
    "e_down": "TensorE: a pair's output", "y_sb": "ScalarE: in SBUF", "pooled": "VectorE: a pooled group",
}

TAKES = {
    "recip": "b_z", "m_sp": "b_z", "m_cols": "b_f", "m_log": "b_diff", "m_ss": "b_qd", "r_sub": "g_diff",
    "m_raw": "b_ez", "m_ln": "b_lf", "m_b_sb": "g_gates_sb", "m_ws": "b_decay", "m_exp": "g_decay", "hi": "g_decay",
    "m_rs": "g_kdf", "r_exp": "g_ln", "r_affT_sb": "g_cols", "r_thr_sb": "g_k_sb", "e_exp": "ff_exp",
    "m_gates": "g_gates", "m_tok": "b_v", "m_b": "b_kdT", "m_wT": "g_t", "r_tok": "g_v",
    "r_affT": "g_cum", "r_thr_rows": "g_k", "half_used": "g_k", "x_sel": "g_vn",
    "m_rows": "b_score", "m_ds": "b_ds", "m_qk": "g_r", "w_att": "g_r", "m_inter": "g_brows", "m_num": "g_score",
    "m_w": "g_rhs", "lo": "g_rhs", "m_kw": "g_al",
}


def build(nc, args, out, par):
    a = args
    general, first_t, even_t, pool_t = (packed(t)[1] for t in constants())
    with ExitStack() as ctx:
        sizes = {"ring": RING * PANEL, "consts": general["freq"][1], "stage_tables": pool_t["count16"][1],
                 "params": par["final"][1], "x": KB * T, "h": KB * T, "mix": KB * T, "proj": 23 * T, "work": 15 * T,
                 "small": 640}

        def place(into, suffix, dtype):
            return {name: into.enter_context(nc.sbuf_tensor(name + suffix, [P, n], dtype)) for name, n in sizes.items()}

        with ExitStack() as plain_names:
            plain = place(plain_names, "", F32)
        halves_of = place(ctx, "_halves", F32R)
        ring, consts, stage_tables, params = (plain[n] for n in ("ring", "consts", "stage_tables", "params"))
        x, h, mix = (plain[n].rearrange("p (k t) -> p k t", k=KB) for n in ("x", "h", "mix"))
        proj_all, work, small = (plain[n] for n in ("proj", "work", "small"))
        proj = proj_all[:, :].rearrange("p (k t) -> p k t", k=23)
        ps = ctx.enter_context(nc.psum_tensor("ps", [P, 8, 512], F32))
        sem = {name: ctx.enter_context(nc.semaphore(name)) for name in SIGNALS if name not in TAKES}
        sem |= {name: sem[other] for name, other in TAKES.items()}
        slot_in = [ctx.enter_context(nc.semaphore(f"slot_in{r}")) for r in range(RING)]

        def const(name):
            return consts[:, general[name][0]:general[name][1]]

        def table(where, name):
            return stage_tables[:, where[name][0]:where[name][1]]

        def param(name, k=None):
            lo, hi = par[name]
            return params[:, lo:hi] if k is None else params[:, lo + k:lo + k + 1]

        def cut(buffer, start, size, **shape):
            v = buffer[:, start:start + size]
            if not shape:
                return v
            names_ = " ".join(shape)
            return v.rearrange(f"p ({names_}) -> p {names_}", **shape)

        cond = cut(small, 0, 8 * 8, v=8, k=8)
        mod = cut(small, 64, 96, w=2, v=6, k=8)
        coef = cut(small, 160, 32, w=4, k=8)
        stats = small[:, 192:640]
        creps = [cut(work, at, KB * 32, k=KB, r=32) for at in (0, 768)]
        mod_rows = cut(work, 256, 512, b=2, n=256)
        hflat = h.rearrange("p k t -> p (k t)")
        ones, ident, halves = const("ones"), const("ident"), const("halves")

        def two(buffer, at):
            return cut(buffer, at, 2 * T, b=2, t=T)

        def four(buffer, at):
            return cut(buffer, at, 4 * T, h=4, t=T)

        hbuf = h.rearrange("p k t -> p (k t)")
        sq, rstd = two(work, 1024), two(work, 2048)
        cos_t, sin_t = work[:, 0:T], work[:, T:2 * T]
        rope_a, rope_b = two(work, 3072), two(work, 4096)
        gn_sq, gn_rstd = sq, rstd
        krep = work[:, 5120:5120 + 2 * 640].rearrange("p (g t) -> p g t", g=2)
        prob = hbuf[:, 0:2048].rearrange("p (i n k) -> p i n k", i=2, n=4)
        probT = cut(hbuf, 2048, 1024, j=8, q=P)
        vtok, w_tok = cut(hbuf, 3072, 512, n=4, f=P), cut(work, 0, 2048, n=4, f=T)
        positions = rope_b[:, 0, :].bitcast(I32)
        b_cum, b_e, b_d = (two(hbuf, 1024 * i) for i in range(3))
        b_q, b_k = (two(hbuf, 3072), two(work, 5632)), (two(work, 0), two(work, 6656))
        b_at = four(work, 1024)
        b_vt, b_kdt = cut(work, 3072, 1024, c=4, f=256), cut(work, 4096, 1024, c=4, f=256)
        b_s, b_tmp = cut(work, 5120, 256, b=2, e=P), cut(work, 5376, 256, b=2, e=P)
        g_A, g_T, g_Y = (four(work, 2048 * i) for i in range(3))
        g_X = four(proj_all, 2048)
        g_vt, g_kdt = cut(proj_all, 4096, 1024, c=4, f=256), cut(proj_all, 5120, 1024, c=4, f=256)
        g_kb = two(proj_all, 6144)
        g_qk, g_L = four(hbuf, 0), four(hbuf, 2048)
        g_al = (four(proj_all, 0), g_L)
        g_eg = two(proj_all, 0)
        g_s = cut(work, 7168, 256, b=2, e=P)
        g_rhs, g_vnew, g_stmp = work[:, 7424:7680], work[:, 6144:6400], cut(work, 6400, 256, b=2, e=P)
        g_g, g_beta, g_gt, g_tot, g_kdf, g_last = (stats[:, 64 + 16 * i:80 + 16 * i] for i in range(6))
        g_sp = stats[:, 160:224]

        mixflat = mix.rearrange("p k t -> p (k t)")
        x_ctx, h_ctx = cut(mixflat, 2048, 2048, k=KB, t=TC), cut(mixflat, 0, 2048, k=KB, t=TC)

        def ctx_proj(i):
            if 2 <= i < 10:
                return mixflat[:, 2048 + (i - 2) * TC:2048 + (i - 1) * TC]
            at = even_t["mask_b"][1] + {0: 0, 1: 1, 10: 2}[i] * TC
            return stage_tables[:, at:at + TC]

        e_krep, e_vtok = cut(hbuf, 0, 1536, g=2, t=768), cut(hbuf, 1536, 768, j=6, f=P)
        e_prob, e_probT = cut(work, 0, 1536, i=2, k=768), cut(work, 1536, 1536, i=2, j=6, q=P)
        e_tok = cut(work, 3072, 2048, n=4, f=T)
        m_kt, m_vt = cut(hbuf, 0, 3072, j=6, f=T), cut(work, 0, 3072, j=6, f=T)
        m_wT, m_z = cut(hbuf, 3072, 1024, i=8, t=P), cut(work, 3072, 1024, i=8, e=P)
        m_h = cut(work, 4096, 2048, j=4, f=T)
        m_wt_raw, m_kw, m_tmp = (cut(proj_all, 1024 * i, 1024, i=8, t=P) for i in range(3))
        m_raw = stats[:, 0:96]
        m_ig, m_lf, m_b, m_a, m_tot = (cut(stats, 96 + 48 * i, 48, d=2, n=24) for i in range(5))
        (m_n, m_prev, m_M, m_end, m_neg, m_wi, m_floor, m_ws, m_dec, m_rs, m_rm, m_am, m_u, m_v) = (
            stats[:, 336 + 8 * i:344 + 8 * i] for i in range(14))
        r_aff, r_gt, r_eq, r_sel, r_slot, r_tmp = (cut(stats, 64 * i, 64, n=4, e=E) for i in range(6))
        r_top, r_need, r_max, r_thr = stats[:, 384:392], stats[:, 392:408], stats[:, 408:412], stats[:, 412:428]
        r_affT, r_thr_rows = two(work, 6144), work[:, 7168:7296]
        h_tok, sel = cut(mixflat, 0, 4096, n=4, f=D), cut(work, 0, 4096, n=4, c=D)
        r_pg, x_sel, e_act = work[:, 6144:7168], cut(work, 4096, 1024, k=KB, c=P), work[:, 5120:6144]
        r_pgT, y_store = cut(hbuf, 0, 4096, i=8, t=T), cut(proj_all, 0, 8192, i=8, d=D)
        e_actT, e_tmp = cut(proj_all, 8192, 1024, k=KB, c=P), proj_all[:, 9216:10240]

        panels = []

        halved = []

        def by_columns(w, n, width=256, halve=False):
            for n0 in range(0, n, width):
                n1 = min(n0 + width, n)
                if halve:
                    halved.append(len(panels))
                panels.append((w[:, n0:n1].rearrange("(k p) n -> p k n", p=P), KB, n1 - n0))

        def by_rows(w, rows_, half):
            for k0 in range(0, rows_, 4):
                k1 = min(k0 + 4, rows_)
                v = w[k0 * P:k1 * P, half * 512:half * 512 + 512]
                halved.append(len(panels))
                panels.append((v.rearrange("(k p) n -> p k n", p=P), k1 - k0, 512))

        def modulation_panels(plan):
            for vec in plan:
                by_columns(a[vec.weights][vec.layer][:, vec.v * D:(vec.v + 1) * D], D)

        modulation_panels(PLANS["start"])
        for l in range(2):
            by_columns(a["w_in"][l], 2824, halve=True)
            modulation_panels(PLANS[f"layer{l}"])
            by_columns(a["w_out"][l], D, halve=True)
            for j in range(0, FF, 256):
                by_columns(a["w_gate"][l][:, j:j + 256], 256, halve=True)
                by_columns(a["w_up"][l][:, j:j + 256], 256, halve=True)
            for half in range(2):
                by_rows(a["w_down"][l], FB, half)

        def expert_panels(l):
            for e in range(0, E, 2):
                for w in ("w_exp_gate", "w_exp_up", "w_exp_down"):
                    for j in range(4):
                        for s in range(2):
                            v = a[w][l, e + s, 2 * j * P:(2 * j + 2) * P, :]
                            panels.append((v.rearrange("(k p) n -> p k n", p=P), 2, D))

        by_columns(a["w_in_even"][0], 2832)
        modulation_panels(PLANS["even"])
        by_columns(a["w_out_even"][0], D, halve=True)
        expert_panels(0)
        by_columns(a["w_in_odd"][0], D, halve=True)
        panels.append((a["w_pool_grp"][0].rearrange("g (k p) e -> p (g k) e", p=P), KB, 256))
        expert_panels(1)

        def slot(n):
            _, k, width = panels[n]
            return cut(ring, n % RING * PANEL, k * width, k=k, n=width)

        panel_hi = [cut(work, at, PANEL) for at in (5120, 1024)]

        def panel_high(s):
            _, k, width = panels[halved[s]]
            return cut(panel_hi[s % 2], 0, k * width, k=k, n=width)

        def ff_high(k):
            if 4 <= k < 20:
                return (mix if k < 12 else h)[:, (k - 4) % 8, :]
            at = {0: 4096, 1: 4608, 2: 0, 3: 512, 20: 3072, 21: 3584}[k]
            return work[:, at:at + T]

        down_panels = 2 * (-(-FB // 4))

        def rounded(v):
            return bass.AP(tensor=halves_of[v.tensor.name], offset=v.offset, ap=v.ap)

        combining = {3: (range(0, 3), range(0, 4)), 4: (range(0, 3), range(4, 8)),
                     6: (range(3, 6), range(0, 4)), 7: (range(3, 6), range(4, 8))}
        gate_tiles = {0: (0, 1), 1: (2, 3)}
        last_pairs = range(6, 8)

        def make_link(eng, name):
            count = [0]

            def link(ins):
                count[0] += 1
                ins.then_inc(sem[name], 1)
                eng.wait_ge(sem[name], count[0])
            return link

        block = ctx.enter_context(nc.Block())

        @block.sync
        def _(sp):
            for n, (src, k, width) in enumerate(panels):
                if n >= RING:
                    sp.wait_ge(sem["panel_used"], n - RING + 1)
                sp.dma_start(slot(n), src).then_inc(slot_in[n % RING], 16)
                if n == 0:
                    sp.dma_start(x, a["xT"].rearrange("(k p) t -> p k t", p=P)).then_inc(sem["x_in"], 16)

        @block.tensor
        def _(pe):
            due = Due(sem)
            at, free, splits = [0], [0], [0]

            def mm(o, lhsT, rhs, start, stop, signal=None, **kw):
                i = pe.matmul(o, lhsT, rhs, start=start, stop=stop, **kw)
                if signal:
                    i.then_inc(sem[signal], 1)
                elif free[0]:
                    i.then_inc(sem["panel_used"], free[0])
                    free[0] = 0

            def mm3(o, lhs, rhs, start, stop, signal=None, used=None):
                mm(o, rounded(lhs[0]), rounded(rhs[0]), start, False)
                mm(o, rounded(lhs[0]), rounded(rhs[1]), False, False, used)
                mm(o, rounded(lhs[1]), rounded(rhs[0]), False, stop, signal)

            def turn(o, i, signal=None, n=P):
                t = pe.transpose(o, i, ident[0:n, 0:n])
                if signal:
                    t.then_inc(sem[signal], 1)

            def panel():
                n = at[0]
                at[0] += 1
                pe.wait_ge(slot_in[n % RING], 16 * (n // RING + 1))
                return slot(n)

            def halved_panel():
                w = panel()
                pe.wait_ge(*due("lo"))
                splits[0] += 1
                return panel_high(splits[0] - 1), w

            def modulation(name):
                plan = PLANS[name]
                pe.wait_ge(*due("cond"))
                for i, vec in enumerate(plan):
                    w = [panel() for _ in range(4)]
                    for k in range(KB):
                        for g in range(4):
                            if k == KB - 1 and g == 2:
                                free[0] += 3
                            mm(ps[32 * g:32 * g + 32, i % 2, 0:256], creps[vec.cond][:, k, :], w[g][:, k, :],
                               k == 0, k == KB - 1, "mod_row" if k == KB - 1 and g == 3 else None)
                    free[0] += 1
                    if i:
                        mod_columns(i - 1)
                mod_columns(len(plan) - 1)
                due("mod_ready", 2)

            def mod_columns(i):
                pe.wait_ge(*due("mod_sb"))
                if i >= 2:
                    pe.wait_ge(*due("mod_ready"))
                for j in range(2):
                    turn(ps[:, 2 + i % 2, j * P:j * P + P], mod_rows[:, i % 2, j * P:j * P + P],
                         "mod_tr" if j else None)

            def norm(t=T):
                for k in range(KB):
                    pe.wait_ge(*due("sq"))
                    mm(ps[:, 4, 0:t], ones, sq[:, k % 2, 0:t], k == 0, k == KB - 1, "sq_sum")

            def project_halved(blocks, rhs, tail=0, signal="lin", used="proj"):
                width_ = blocks + (tail > 0)
                for m in range(width_):
                    width = P if m < blocks else tail
                    if m % 2 == 0:
                        if m:
                            free[0] += 1
                        w = halved_panel()
                    if m >= 4:
                        pe.wait_ge(*due(used))
                    s = slice(m % 2 * P, m % 2 * P + width)
                    for k in range(KB):
                        if m == 0:
                            pe.wait_ge(*due("lo"))
                        mm3(ps[0:width, m % 4, :], (w[0][:, k, s], w[1][:, k, s]), (rhs[0][:, k, :], rhs[1][:, k, :]),
                            k == 0, k == KB - 1, signal if k == KB - 1 else None,
                            "half_used" if signal == "y" and m % 2 and k == KB - 1 else None)
                free[0] += 1
                due(used, min(4, width_))

            def head_norm(n, t=T):
                for b in range(n):
                    pe.wait_ge(*due("gn_sq"))
                    mm(ps[:, 4 + b % 2, 0:t], halves, gn_sq[:, b % 2, 0:t], True, True, "gn_sum")
                due("gn", n)

            def rope(n, rot):
                def rotate(b):
                    pe.wait_ge(*due("gn"))
                    if b >= 2:
                        pe.wait_ge(*due("roped"))
                    mm(ps[:, 6 + b % 2, :], rot, proj[:, b, :], True, True, "rot")

                for b in range(n):
                    pe.wait_ge(*due("gn_sq"))
                    mm(ps[:, 4 + b % 2, :], halves, gn_sq[:, b % 2, :], True, True, "gn_sum")
                    if b:
                        rotate(b - 1)
                rotate(n - 1)
                due("roped", 2)

            def windows():
                for g in range(2):
                    mm(ps[:, g, :], const(f"dup{g}"), proj[:, 4, :], True, True, "krep")
                for n in range(NT):
                    turn(ps[:, 7, n * P:n * P + P], proj[:, 5, n * P:n * P + P], "vt" if n == NT - 1 else None)
                pe.wait_ge(*due("krep_sb", 2))
                pe.wait_ge(*due("krep_pad"))
                pe.wait_ge(*due("vt_sb"))

                def scores(hd):
                    q = slice(hd % 2 * 64, hd % 2 * 64 + 64)
                    if hd >= 2:
                        pe.wait_ge(*due("smax"))
                    for n in range(NT):
                        mm(ps[:, hd % 2 * 2 + n // 2, n % 2 * 256:n % 2 * 256 + 256],
                           proj[q, hd // 2, n * P:n * P + P], krep[q, hd // 4, n * P:n * P + 256],
                           True, True, "score" if n == NT - 1 else None)

                def turns(hd):
                    pe.wait_ge(*due("pexp"))
                    for n in range(NT):
                        for j in range(2):
                            turn(ps[:, 4 + n // 2, (n % 2 * 2 + j) * P:(n % 2 * 2 + j) * P + P],
                                 prob[:, hd % 2, n, j * P:j * P + P], "probT" if n == NT - 1 and j else None)

                def output(hd):
                    pe.wait_ge(*due("probT_sb"))
                    if hd >= 2:
                        pe.wait_ge(*due("w_mixed"))
                    for n in range(NT):
                        for j in range(0 if n else 1, 2):
                            mm(ps[:, 6 + hd % 2, n * 64:n * 64 + 64], probT[:, 2 * n + j, :],
                               vtok[:, n - 1 + j, hd // 4 * 64:hd // 4 * 64 + 64],
                               j == (0 if n else 1), j == 1, "w_att" if n == NT - 1 and j else None)

                scores(0)
                scores(1)
                for hd in range(8):
                    if hd < 6:
                        scores(hd + 2)
                    if hd:
                        output(hd - 1)
                    turns(hd)
                output(7)
                due("smax", 2)
                pe.wait_ge(*due("w_mixed", 2))
                to_features(w_tok)

            def to_features(v):
                for b in range(4):
                    for n in range(NT):
                        turn(ps[:, b, n * P:n * P + P], v[:, n, b * P:b * P + P], "att" if n == NT - 1 else None)

            def chunk_turns(src, n, banks, signal):
                for b in range(n):
                    for c in range(NT):
                        turn(ps[:, banks + c // 2, (c % 2 * 2 + b) * P:(c % 2 * 2 + b) * P + P],
                             src[:, b, c * P:c * P + P], signal if b == n - 1 and c == NT - 1 else None)

            def hgrn():
                chunk_turns(proj[:, 10:12, :], 2, 4, "b_v")
                for n in range(len(LEVELS) + 1):
                    pe.wait_ge(*due("b_qk"))
                    if n == 1:
                        pe.wait_ge(*due("b_v_sb"))
                    for hd in range(H1):
                        r = slice(hd % 2 * 64, hd % 2 * 64 + 64)
                        q = proj[r, 6 + hd // 2, :] if n == 0 else b_q[n % 2][r, hd // 2, :]
                        k = proj[r, 8 + hd // 2, :] if n == 0 else b_k[n % 2][r, hd // 2, :]
                        if n >= 2:
                            pe.wait_ge(*due("b_acc"))
                        for c in range(NT):
                            mm(ps[:, n % 2 * 4 + hd, c * P:c * P + P], k[:, c * P:c * P + P], q[:, c * P:c * P + P],
                               True, True, "b_score" if c == NT - 1 else None)
                pe.wait_ge(*due("b_acc", 2 * H1))
                pe.wait_ge(*due("b_kd"))
                chunk_turns(b_d, 2, 4, "b_kdT")
                pe.wait_ge(*due("b_kdT_sb"))
                pe.wait_ge(*due("b_acc", 0))
                for c in range(NT):
                    pe.wait_ge(*due("b_state"))
                    cs = slice(c * P, c * P + P)
                    for b in range(2):
                        for s in range(2):
                            r = slice(s * 64, s * 64 + 64)
                            mm(ps[r, b, cs], b_s[:, b, r], b_e[:, b, cs], True, False)
                            mm(ps[r, b, cs], b_vt[:, c, b * P + s * 64:b * P + s * 64 + 64], b_at[:, 2 * b + s, cs],
                               False, True)
                    if c < NT - 1:
                        for b in range(2):
                            mm(ps[:, 4, b * P:b * P + P], b_kdt[:, c, b * P:b * P + P], b_vt[:, c, b * P:b * P + P],
                               True, True, "b_ds" if b else None)
                mm(ps[:, 5, 0:P], ident, ident, True, True, "b_out")

            def delta():
                for c in range(NT):
                    turn(ps[:, 7, c * 8:c * 8 + 8], proj[0:8, 22, c * P:c * P + P], "g_gates" if c == NT - 1 else None, 8)
                chunk_turns(proj[:, 18:20, :], 2, 4, "g_v")
                pe.wait_ge(*due("g_g"))
                mm(ps[:, 7, 64:80], const("upto"), g_g, True, True)
                mm(ps[:, 7, 96:112], ones, g_g, True, True, "g_cum")
                for hd in range(H1):
                    for c in range(NT):
                        mm(ps[:, hd, c * P:c * P + P], g_g[:, hd * 4 + c:hd * 4 + c + 1].to_broadcast([P, P]),
                           const("upto"), True, True, "g_rows" if c == NT - 1 else None)
                pe.wait_ge(*due("g_eg", H1))
                pe.wait_ge(*due("g_diffs", H1))
                for hd in range(H1):
                    for c in range(NT):
                        mm(ps[:, hd, c * P:c * P + P], g_beta[:, hd * 4 + c:hd * 4 + c + 1].to_broadcast([P, P]),
                           ident, True, True, "g_brows" if c == NT - 1 else None)
                pe.wait_ge(*due("g_v_raw"))
                chunk_turns(proj[:, 16:18, :], 2, 4, "g_k")
                for n in range(2):
                    if n == 0:
                        pe.wait_ge(*due("g_kb"))
                    for hd in range(H1):
                        r = slice(hd % 2 * 64, hd % 2 * 64 + 64)
                        rhs = (g_kb if n == 0 else proj[:, 14:16, :])[r, hd // 2, :]
                        if n:
                            pe.wait_ge(*due("g_acc"))
                        for c in range(NT):
                            mm(ps[:, hd, c * P:c * P + P], proj[r, 16 + hd // 2, c * P:c * P + P],
                               rhs[:, c * P:c * P + P], True, True, "g_score" if c == NT - 1 else None)
                pe.wait_ge(*due("g_acc", H1))
                pe.wait_ge(*due("g_y"))
                for hd in range(H1):
                    for c in range(NT):
                        turn(ps[:, hd, c * P:c * P + P], g_Y[:, hd, c * P:c * P + P], "g_t" if c == NT - 1 else None)
                pe.wait_ge(*due("g_t_sb", H1))
                for n, s in enumerate(reversed(LEVELS[:-1])):
                    last = s == LEVELS[0]
                    for half in range(2):
                        pe.wait_ge(*due("g_al"))
                        for hd in (2 * half, 2 * half + 1):
                            for c in range(NT):
                                cs = slice(c * P, c * P + P)
                                mm(ps[:, hd, cs], g_al[n % 2][:, hd, cs], g_T[:, hd, cs], True, True,
                                   "g_x" if c == NT - 1 else None)
                    for half in range(2):
                        for hd in (2 * half, 2 * half + 1):
                            pe.wait_ge(*due("g_x_sb"))
                        for hd in (2 * half, 2 * half + 1):
                            if half:
                                pe.wait_ge(*due("g_yt"))
                            for c in range(NT):
                                cs = slice(c * P, c * P + P)
                                mm(ps[:, 4 + hd % 2, cs], g_X[:, hd, cs], g_Y[:, hd, cs], True, True,
                                   "g_dy" if c == NT - 1 else None)
                        if not last:
                            for hd in (2 * half, 2 * half + 1):
                                if half:
                                    pe.wait_ge(*due("g_tt"))
                                for c in range(NT):
                                    cs = slice(c * P, c * P + P)
                                    mm(ps[:, 6 + hd % 2, cs], g_Y[:, hd, cs], g_X[:, hd, cs], True, True,
                                       "g_dt" if c == NT - 1 else None)
                    pe.wait_ge(*due("g_yt", 2))
                    if not last:
                        pe.wait_ge(*due("g_tt", 2))
                for c in range(NT):
                    cs = slice(c * P, c * P + P)
                    pe.wait_ge(*due("g_state"))
                    for b in range(2):
                        mm(ps[:, 0, b * P:b * P + P], g_kb[:, b, cs], g_s[:, b, :], True, True, "g_r" if b else None)
                    pe.wait_ge(*due("g_rhs"))
                    for hd in range(H1):
                        mm(ps[:, 1, hd * 64:hd * 64 + 64], g_Y[:, hd, cs], g_rhs[:, hd * 64:hd * 64 + 64],
                           True, True, "g_vn" if hd == H1 - 1 else None)
                    pe.wait_ge(*due("g_vn_sb"))
                    for b in range(2):
                        for s in range(2):
                            r = slice(s * 64, s * 64 + 64)
                            mm(ps[r, 2 + b, cs], g_s[:, b, r], proj[:, 14 + b, cs], True, False)
                            mm(ps[r, 2 + b, cs], g_vnew[:, b * P + s * 64:b * P + s * 64 + 64], g_qk[:, 2 * b + s, cs],
                               False, True)
                    for b in range(2):
                        mm(ps[:, 4, b * P:b * P + P], g_kdt[:, c, b * P:b * P + P], g_vnew[:, b * P:b * P + P],
                           True, True, "g_ds" if b else None)

            def swiglu():
                for jj in range(FB // 2):
                    if jj >= 2:
                        pe.wait_ge(*due("ff", 2))
                    for s in range(2):
                        w = halved_panel()
                        for j in range(2):
                            for k in range(KB):
                                if jj == s == j == 0:
                                    pe.wait_ge(*due("lo"))
                                mm3(ps[:, jj % 2 * 4 + 2 * s + j, :], (w[0][:, k, j * P:j * P + P], w[1][:, k, j * P:j * P + P]),
                                    (mix[:, k, :], h[:, k, :]), k == 0, k == KB - 1, "gu" if k == KB - 1 else None)
                        free[0] += 1
                pe.wait_ge(*due("ff", 2))
                for half in range(2):
                    if half:
                        pe.wait_ge(*due("ff", 2))
                    for k0 in range(0, FB, 4):
                        w = halved_panel()
                        for k in range(k0, min(k0 + 4, FB)):
                            if half == 0:
                                pe.wait_ge(*due("lo"))
                            for m in range(4):
                                s = slice(m * P, m * P + P)
                                mm3(ps[:, 4 - 4 * half + m, :], (w[0][:, k - k0, s], w[1][:, k - k0, s]),
                                    (ff_high(k), proj[:, k, :]), k == 0, k == FB - 1, "down" if k == FB - 1 else None,
                                    "half_used" if m == 3 and k in (k0 + 3, FB - 1) else None)
                        free[0] += 1

            def barrier():
                pe.drain().then_inc(sem["stage"], 1)
                pe.wait_ge(*due("stage", 3))

            def project_even():
                n_c = 0
                for m in range(23):
                    width = P if m < 22 else 16
                    if m % 2 == 0:
                        if m:
                            free[0] += 1
                        w = panel()
                    if m >= 4:
                        pe.wait_ge(*due("proj"))
                    for k in range(KB):
                        if m == k == 0:
                            pe.wait_ge(*due("h", 2 * KB))
                        mm(ps[0:width, m % 4, :], w[:, k, m % 2 * P:m % 2 * P + width], h[:, k, :],
                           k == 0, k == KB - 1, "lin" if k == KB - 1 else None)
                    if m in CTX_BLOCKS:
                        if n_c >= 4:
                            pe.wait_ge(*due("proj_c"))
                        for k in range(KB):
                            mm(ps[0:width, 4 + n_c % 4, 0:TC], w[:, k, m % 2 * P:m % 2 * P + width], h_ctx[:, k, :],
                               k == 0, k == KB - 1, "lin_c" if k == KB - 1 else None)
                        n_c += 1
                free[0] += 1
                due("proj", 4)
                due("proj_c", 4)

            def attention():
                for g in range(2):
                    mm(ps[:, g, :], const(f"dup{g}"), proj[:, 4, :], True, True, "krep")
                    mm(ps[:, 2 + g, 0:TC], const(f"dup{g}"), ctx_proj(0), True, True, "krep")
                for j in range(6):
                    src = ctx_proj(1)[:, j * P:j * P + P] if j < 2 else proj[:, 5, (j - 2) * P:(j - 1) * P]
                    turn(ps[:, 4 + j // 4, j % 4 * P:j % 4 * P + P], src, "vt" if j == 5 else None)
                pe.wait_ge(*due("krep_sb", 4))
                pe.wait_ge(*due("vt_sb"))

                def scores(i):
                    hd, n = i // NT, i % NT
                    r = slice(hd % 2 * 64, hd % 2 * 64 + 64)
                    for b, (lo, hi) in enumerate(((0, 512), (512, 768))):
                        mm(ps[:, i % 2 * 2 + b, 0:hi - lo], proj[r, hd // 2, n * P:n * P + P],
                           e_krep[r, hd // 4, lo:hi], True, True, "score" if b else None)

                def turns(i):
                    if i >= 2:
                        pe.wait_ge(*due("mixed"))
                    bank = 4 + i % 2 * 2
                    for j in range(6):
                        turn(ps[:, bank + j // 4, j % 4 * P:j % 4 * P + P], e_prob[:, i % 2, j * P:j * P + P],
                             "probT" if j == 5 else None)

                def output(i):
                    pe.wait_ge(*due("probT_sb"))
                    for j in range(6):
                        mm(ps[:, 5 + i % 2 * 2, 256:384], e_probT[:, i % 2, j, :], e_vtok[:, j, :],
                           j == 0, j == 5, "att" if j == 5 else None)

                tiles = 8 * NT
                scores(0)
                scores(1)
                for i in range(tiles):
                    pe.wait_ge(*due("pexp"))
                    if i < tiles - 2:
                        scores(i + 2)
                    turns(i)
                    if i:
                        output(i - 1)
                output(tiles - 1)
                pe.wait_ge(*due("mixed", 2))
                to_features(e_tok)

            def mlstm():
                for j in range(6):
                    src = ctx_proj(10)[0:16, j * P:j * P + P] if j < 2 else proj[0:16, 22, (j - 2) * P:(j - 1) * P]
                    turn(ps[:, 7, j * 16:j * 16 + 16], src, "m_gates" if j == 5 else None, 16)
                for what in range(2):
                    for j in range(6):
                        if what or j >= 4:
                            pe.wait_ge(*due("m_tok_sb"))
                        for b in range(4):
                            blk = (6 if what == 0 else 2) + b
                            full = (14 if what == 0 else 10) + b
                            src = ctx_proj(blk)[:, j * P:j * P + P] if j < 2 else proj[:, full, (j - 2) * P:(j - 1) * P]
                            turn(ps[:, j % 4 if what == 0 else (j + 2) % 4, b * P:b * P + P], src, "m_tok" if b == 3 else None)
                due("m_tok_sb", 4)
                pe.wait_ge(*due("m_lf"))
                for d, which in enumerate(("upto", "from")):
                    mm(ps[:, 6, d * 32:d * 32 + 24], const(which), m_lf[:, d, :], True, True)
                    mm(ps[:, 6, 64 + d * 32:64 + d * 32 + 24], ones, m_lf[:, d, :], True, True, "m_b" if d else None)
                pe.wait_ge(*due("m_a"))
                for step in range(6):
                    tiles = (step, M_BACK[step])
                    if step:
                        pe.wait_ge(*due("m_state"))
                    for i in range(8):
                        col = m_a[:, i // 4, tiles[i // 4] * 4 + i % 4:tiles[i // 4] * 4 + i % 4 + 1]
                        mm(ps[:, i // 4, i % 4 * P:i % 4 * P + P], col.to_broadcast([P, P]), ident, True, True,
                           "m_rows" if i == 7 else None)
                    if step >= 2:
                        for i in range(8):
                            t0 = (tiles[i // 4] - 2) * P
                            mm(ps[:, 2 + i // 4, i % 4 * P:i % 4 * P + P], proj[:, 6 + i % 4, t0:t0 + P],
                               proj[:, 10 + i % 4, t0:t0 + P], True, True, "m_qk" if i == 7 else None)
                        for i in range(8):
                            t0 = (tiles[i // 4] - 2) * P
                            mm(ps[:, 6 + i // 4, i % 4 * P:i % 4 * P + P], proj[:, 6 + i % 4, t0:t0 + P], m_z[:, i, :],
                               True, True)
                        pe.wait_ge(*due("m_w"))
                        for i in range(8):
                            turn(ps[:, i // 4, i % 4 * P:i % 4 * P + P], m_wt_raw[:, i, :], "m_wT" if i == 7 else None)
                        for i in range(8):
                            t0 = (tiles[i // 4] - 2) * P
                            mm(ps[:, 2, i:i + 1], proj[:, 6 + i % 4, t0:t0 + P], m_n[:, i:i + 1], True, True,
                               "m_inter" if i == 7 else None)
                        pe.wait_ge(*due("m_wT_sb"))
                        for i in range(8):
                            mm(ps[:, 4 + i // 4, i % 4 * P:i % 4 * P + P], m_wT[:, i, :],
                               m_vt[:, tiles[i // 4], i % 4 * P:i % 4 * P + P], True, True, "m_num" if i == 7 else None)
                    if step < 5:
                        pe.wait_ge(*due("m_kw"))
                        for i in range(8):
                            mm(ps[:, i // 4, i % 4 * P:i % 4 * P + P], m_kw[:, i, :],
                               m_vt[:, tiles[i // 4], i % 4 * P:i % 4 * P + P], True, True)
                        for i in range(8):
                            mm(ps[:, 3, i:i + 1], m_kw[:, i, :], ones[:, 0:1], True, True, "m_ds" if i == 7 else None)
                pe.wait_ge(*due("m_h"))
                for hd in range(4):
                    for j in range(4):
                        turn(ps[:, hd, j * P:j * P + P], m_h[:, j, hd * P:hd * P + P], "m_hT" if j == 3 else None)

            def experts(l):
                for k in range(KB):
                    pe.wait_ge(*due("h"))
                for n in range(NT):
                    for k in range(KB):
                        mm(ps[:, 0, n * E:n * E + E], h[:, k, n * P:n * P + P], param(f"router{l}")[:, k * E:k * E + E],
                           k == 0, k == KB - 1, "r_logits" if n == NT - 1 and k == KB - 1 else None)
                for n in range(NT):
                    for half in range(2):
                        if n:
                            pe.wait_ge(*due("r_tok_sb"))
                        for j in range(4):
                            k = half * 4 + j
                            turn(ps[:, 4 + half, j * P:j * P + P], h[:, k, n * P:n * P + P], "r_tok" if j == 3 else None)
                due("r_tok_sb", 2)
                pe.wait_ge(*due("r_aff"))
                for n in range(NT):
                    turn(ps[0:E, 1, n * P:n * P + P], r_aff[:, n, :], "r_affT" if n == NT - 1 else None)
                pe.wait_ge(*due("r_thr"))
                turn(ps[:, 2, 0:E], r_thr_rows[0:E, :], "r_thr_rows", E)
                for what in ("ties", "taken"):
                    pe.wait_ge(*due("r_marks"))
                    marks = r_eq if what == "ties" else r_sel
                    for n in range(NT):
                        for j in range(n + 1):
                            mm(ps[:, 3, n * E:n * E + E], const("upto") if j == n else ones, marks[:, j, :],
                               j == 0, j == n, "r_count" if what == "taken" and j == n == NT - 1 else None)
                    if what == "ties":
                        for n in range(NT):
                            mm(ps[:, 3, 64:64 + E], ones, r_gt[:, n, :], n == 0, n == NT - 1,
                               "r_count" if n == NT - 1 else None)

                def turn_gates(tiles):
                    for n in tiles:
                        pe.wait_ge(*due("r_pg"))
                        for p in range(8):
                            turn(ps[:, 6 + p // 4, p % 4 * P:p % 4 * P + P], r_pg[:, p * P:p * P + P],
                                 "r_pgT" if p == 7 else None)
                        pe.wait_ge(*due("r_pgT_sb"))

                def gather(p):
                    for m in range(KB):
                        for n in range(NT):
                            mm(ps[:, 6 + m // 4, m % 4 * P:m % 4 * P + P], h_tok[:, n, m * P:m * P + P],
                               sel[:, n, p * P:p * P + P], n == 0, n == NT - 1,
                               "x_sel" if m == KB - 1 and n == NT - 1 else None)

                def pair(banks, lhs, signal):
                    for j in range(4):
                        w = [panel(), panel()]
                        for kk in range(2):
                            k = 2 * j + kk
                            for half in range(2):
                                for e in range(2):
                                    s = slice(e * 64, e * 64 + 64)
                                    mm(ps[s, banks + half, :], lhs[:, k, s], w[e][:, kk, half * 512:half * 512 + 512],
                                       k == 0, k == KB - 1, signal if k == KB - 1 and half and e else None)
                        free[0] += 2

                unread = [0]

                def combine(pairs, m, bank):
                    for p in pairs:
                        mm(ps[:, bank, :], y_store[:, p, m * P:m * P + P], r_pgT[:, p, :], p == pairs[0], p == pairs[-1],
                           "down" if p == pairs[-1] else None)

                def combine_blocks(pairs, blocks):
                    for m in blocks:
                        if unread[0] == 2:
                            pe.wait_ge(*due("down_x"))
                            unread[0] -= 1
                        combine(pairs, m, 6 + m % 2)
                        unread[0] += 1

                pe.wait_ge(*due("r_marks"))
                gather(0)
                pe.wait_ge(*due("x_sel_sb"))
                for p in range(8):
                    pair(0, x_sel, "e_gate")
                    turn_gates(gate_tiles.get(p, ()))
                    if p:
                        pe.wait_ge(*due("y_sb"))
                    if p in combining:
                        combine_blocks(*combining[p])
                    pair(2, x_sel, "e_up")
                    if p < 7:
                        if unread[0]:
                            pe.wait_ge(*due("down_x", unread[0]))
                            unread[0] = 0
                        gather(p + 1)
                        pe.wait_ge(*due("x_sel_sb"))
                    pe.wait_ge(*due("e_act"))
                    for k in range(KB):
                        turn(ps[:, k // 4, k % 4 * P:k % 4 * P + P], e_act[:, k * P:k * P + P], "aT" if k == KB - 1 else None)
                    pe.wait_ge(*due("aT_sb"))
                    pair(4, e_actT, "e_down")
                pe.wait_ge(*due("y_sb"))
                pe.wait_ge(*due("down_x", unread[0]))
                for m in range(KB):
                    combine(last_pairs, m, m)
                due("down_x", KB)

            def pooling():
                w = panel()
                for g in range(4):
                    pe.wait_ge(*due("pooled"))
                    for m in range(2):
                        for k in range(2):
                            mm(ps[:, 2 * g + m, :], w[:, 2 * g + k, m * P:m * P + P], proj[:, 8 + 2 * g + k, :],
                               k == 0, k == 1, "down" if k else None)
                free[0] += 1

            def layer(l):
                norm()
                due("h", KB)
                project_halved(22, (mix, h), 8)
                barrier()
                rope(5, const("rot_rope"))
                barrier()
                windows()
                barrier()
                hgrn()
                barrier()
                head_norm(2)
                modulation(f"layer{l}")
                barrier()
                head_norm(4)
                barrier()
                delta()
                barrier()
                head_norm(2)
                barrier()
                project_halved(8, (h, mix), signal="y", used="y_used")
                barrier()
                norm()
                due("h", KB)
                swiglu()
                due("down_x", KB)
                barrier()

            modulation("start")
            barrier()
            for l in range(2):
                layer(l)

            def moe_layer(l):
                barrier()
                norm()
                barrier()
                experts(l)
                barrier()

            def even_layer():
                norm()
                barrier()
                norm(TC)
                barrier()
                project_even()
                barrier()
                rope(5, const("rot_axial"))
                barrier()
                head_norm(1, TC)
                barrier()
                attention()
                barrier()
                modulation("even")
                barrier()
                mlstm()
                barrier()
                project_halved(8, (h, mix), signal="y", used="y_used")

            def odd_layer():
                barrier()
                norm()
                due("h", KB)
                project_halved(8, (mix, h))
                barrier()
                pooling()
                due("down_x", 8)

            even_layer()
            moe_layer(0)
            odd_layer()
            moe_layer(1)
            norm()

        @block.scalar
        def _(act):
            due = Due(sem)
            link = make_link(act, "act_step")
            f = act.activation
            act.dma_start(consts[:, :], a["general"]).then_inc(sem["const_in"], 16)
            act.dma_start(params[:, :], a["params"]).then_inc(sem["const_in"], 16)
            act.preload_act_table_set("natural_log_exp_and_others")

            def to(signal, ins):
                ins.then_inc(sem[signal], 1)

            def barrier():
                act.drain().then_inc(sem["stage"], 1)
                act.wait_ge(*due("stage", 3))

            splits = [0]

            def split_panel():
                n = halved[splits[0]]
                act.wait_ge(slot_in[n % RING], 16 * (n // RING + 1))
                to("hi", f(rounded(panel_high(splits[0])), slot(n), ACT.Copy))
                splits[0] += 1

            def split_mix():
                split_panel()
                for k in range(KB):
                    to("hi", f(rounded(h[:, k, :]), mix[:, k, :], ACT.Copy))
                split_panel()
                for _ in range(2):
                    act.wait_ge(*due("half_used"))
                    split_panel()
                due("half_used", 2)

            def conditions(name):
                for w, col in enumerate(sum(CONDITIONS[name], ())):
                    i = f(cond[:, w, :], param(col), ACT.Exp, scale=-1.0)
                to("cond_exp", i)

            def mod_row(i):
                act.wait_ge(*due("mod_row"))
                if i >= 2:
                    act.wait_ge(*due("mod_tr"))
                to("mod_sb", f(mod_rows[:, i % 2, :], ps[:, i % 2, 0:256], ACT.Copy))

            def norm(x_, h_, scale, shift, hi=None):
                if hi is None:
                    due("h", KB)
                t = x_.shape[2]
                for k in range(KB):
                    if k >= 2:
                        act.wait_ge(*due("sq_sum"))
                    to("sq", f(sq[:, k % 2, 0:t], x_[:, k, :], ACT.Square))
                act.wait_ge(*due("sq_sum", 2))
                link(f(rstd[:, 1, 0:t], ps[:, 4, 0:t], ACT.Ln, scale=1.0 / D, bias=EPS))
                to("rstd", f(rstd[:, 0, 0:t], rstd[:, 1, 0:t], ACT.Exp, scale=-0.5))
                for k in range(KB):
                    act.wait_ge(*due("xn"))
                    to("h", f(h_[:, k, :], h_[:, k, :], ACT.Identity, scale=scale[:, k:k + 1],
                              bias=0.0 if shift is None else shift[:, k:k + 1]))
                    if hi is not None:
                        act.wait_ge(*due("h"))
                        to("hi", f(rounded(hi[:, k, :]), h_[:, k, :], ACT.Copy))

            def project_halved(blocks, dst, tail=0):
                n = blocks + (tail > 0)
                for m in range(n):
                    width = P if m < blocks else tail
                    act.wait_ge(*due("lin"))
                    to("proj", f(dst[0:width, m, :], ps[0:width, m % 4, :], ACT.Copy))
                    if m % 2 and m + 3 < n:
                        split_panel()

            def head_norm(src, mean):
                n, t = src.shape[1:]

                def squares(b):
                    to("gn_sq", f(gn_sq[:, b % 2, 0:t], src[:, b, :], ACT.Square))

                squares(0)
                for b in range(n):
                    act.wait_ge(*due("gn_sum"))
                    if b + 1 < n:
                        squares(b + 1)
                    if b >= 2:
                        act.wait_ge(*due("gn"))
                    r = gn_rstd[:, b % 2, 0:t]
                    link(f(r, ps[:, 4 + b % 2, 0:t], ACT.Ln, scale=1.0 / 64 if mean else 1.0, bias=EPS))
                    to("gn_rstd", f(r, r, ACT.Exp, scale=-0.5))
                due("gn", min(n, 2))

            def windows(l):
                for g in range(2):
                    act.wait_ge(*due("krep"))
                    to("krep_sb", f(krep[:, g, P:5 * P], ps[:, g, :], ACT.Copy))
                act.wait_ge(*due("vt"))
                to("vt_sb", f(vtok, ps[:, 7, :].rearrange("p (n f) -> p n f", n=4), ACT.Copy))
                def exponentials(hd):
                    act.wait_ge(*due("smax"))
                    pr, o = prob[:, hd % 2, :, :], 24 * (hd % 2)
                    for n in range(NT):
                        f(pr[:, n, :], pr[:, n, :], ACT.Exp, bias=stats[:, o + 4 + n:o + 5 + n],
                          accum_out=stats[:, o + 8 + n:o + 9 + n])
                    to("pexp", f(stats[:, o + 12:o + 16], stats[:, o + 4:o + 8], ACT.Exp, bias=param(f"sinks{l}", hd)))

                exponentials(0)
                for hd in range(8):
                    if hd < 7:
                        exponentials(hd + 1)
                    act.wait_ge(*due("probT"))
                    to("probT_sb", f(probT, ps[:, 4:6, :].rearrange("p b (j q) -> p (b j) q", j=4), ACT.Copy))
                features_out()

            def features_out():
                for b in range(4):
                    act.wait_ge(*due("att"))
                    f(mix[:, b, :], ps[:, b, :], ACT.Copy)

            def trig():
                act.wait_ge(*due("trig"))
                f(sin_t, rope_a[:, 0, :], ACT.Sin)
                to("trig_sb", f(cos_t, rope_a[:, 1, :], ACT.Sin))
                act.preload_act_table_set("natural_log_exp_and_others")

            def gate_exp(src):
                to("gate_exp", f(two(work, 3072), src, ACT.Exp, scale=-1.0))

            def hgrn():
                act.wait_ge(*due("b_z"))
                to("b_ez", f(proj[:, 8:10, :], proj[:, 8:10, :], ACT.Exp, scale=-1.0))
                act.wait_ge(*due("b_v"))
                to("b_v_sb", f(b_vt, ps[:, 4:6, :].rearrange("p b (c f) -> p (b c) f", c=2), ACT.Copy))
                act.wait_ge(*due("b_f"))
                to("b_lf", f(b_d, proj[:, 8:10, :], ACT.Ln))
                for n in range(len(LEVELS)):
                    act.wait_ge(*due("b_diff"))
                    link(f(b_d, b_d, ACT.Abs))
                    to("b_decay", f(b_e, b_d, ACT.Exp, scale=-1.0))
                act.wait_ge(*due("b_qd"))
                link(f(b_e, b_cum, ACT.Exp))
                to("b_decay", f(b_d, b_d, ACT.Exp, scale=-1.0))
                link(f(stats[:, 32:40].rearrange("p (b c) -> p b c", b=2),
                       b_cum.rearrange("p b (c t) -> p b c t", c=4)[:, :, :, P - 1], ACT.Exp))
                act.wait_ge(*due("b_kdT"))
                to("b_kdT_sb", f(b_kdt, ps[:, 4:6, :].rearrange("p b (c f) -> p (b c) f", c=2), ACT.Copy))
                act.wait_ge(*due("b_out"))
                f(mix[:, 4:6, :], ps[:, 0:2, :], ACT.Copy)

            def delta(l):
                act.wait_ge(*due("g_gates"))
                link(f(g_sp[:, 0:32], ps[:, 7, 0:32], ACT.Copy))
                sp = g_sp[:, 0:32].rearrange("p (c g h) -> p c g h", c=4, g=2)
                beta = g_beta.rearrange("p (h c) -> p c h", c=4)
                link(f(beta, sp[:, :, 0, :], ACT.Exp, scale=-1.0))
                to("g_gates_sb", f(stats[:, 40:44], param(f"a_log{l}"), ACT.Exp))
                act.wait_ge(*due("g_v"))
                to("g_v_raw", f(g_vt, ps[:, 4:6, :].rearrange("p b (c f) -> p (b c) f", c=2), ACT.Copy))
                act.wait_ge(*due("g_sum"))
                link(f(g_kdf, g_g, ACT.Abs))
                link(f(g_kdf, g_kdf, ACT.Exp, scale=-1.0))
                to("g_ln", f(g_kdf, g_kdf, ACT.Ln, bias=1.0))
                act.wait_ge(*due("g_cum"))
                link(f(g_gt, ps[:, 7, 64:80], ACT.Copy))
                link(f(g_tot, ps[:, 7, 96:112], ACT.Copy))
                for s in range(2):
                    r = slice(64 * s, 64 * s + 64)
                    i = f(g_last[r, 0:8].rearrange("p (b c) -> p b c", b=2),
                          ps[r, 7, 96:112].rearrange("p (b s c) -> p b s c", b=2, s=2)[:, :, s, :], ACT.Exp)
                    link(i)
                to("g_cols", f(stats[:, 44:48], stats[:, 40:44], ACT.Copy))
                for hd in range(H1):
                    r = slice(hd % 2 * 64, hd % 2 * 64 + 64)
                    act.wait_ge(*due("g_rows"))
                    to("g_eg", f(g_eg[r, hd // 2, :], ps[r, hd, :], ACT.Exp))
                act.wait_ge(*due("g_diff"))
                to("g_decay", f(g_L, g_L, ACT.Exp))
                act.wait_ge(*due("g_kdiff"))
                to("g_kdf", f(g_kdf, g_kdf, ACT.Exp))
                act.wait_ge(*due("g_k"))
                to("g_k_sb", f(g_kdt, ps[:, 4:6, :].rearrange("p b (c f) -> p (b c) f", c=2), ACT.Copy))
                for hd in range(H1):
                    act.wait_ge(*due("g_t"))
                    to("g_t_sb", f(g_T[:, hd, :], ps[:, hd, :], ACT.Copy))
                for _ in LEVELS[:-1]:
                    for hd in range(H1):
                        act.wait_ge(*due("g_x"))
                        to("g_x_sb", f(g_X[:, hd, :], ps[:, hd, :], ACT.Copy))
                for c in range(NT):
                    act.wait_ge(*due("g_vn"))
                    to("g_vn_sb", f(g_vnew, ps[:, 1, 0:256], ACT.Copy))
                act.wait_ge(*due("g_ds", NT))
                f(mix[:, 6:8, :], ps[:, 2:4, :], ACT.Copy)

            def conv_silu(n):
                for b in range(n):
                    act.wait_ge(*due("conv"))
                    if b >= 2:
                        act.wait_ge(*due("conv_done"))
                    to("conv_exp", f(rope_b[:, b % 2, :], rope_a[:, b % 2, :], ACT.Exp, scale=-1.0))
                    mod_row(b)
                due("conv_done", 2)
                due("mod_tr", 2)

            def swiglu():
                pairs = FB // 2
                for jj in range(pairs):
                    for j in range(2):
                        act.wait_ge(*due("gu"))
                        if jj:
                            act.wait_ge(*due("ff"))
                        to("ff_exp", f(rope_a[:, j, :], ps[:, jj % 2 * 4 + j, :], ACT.Exp, scale=-1.0))
                    split_panel()
                    if jj == pairs - 1:
                        ff_halves(0)
                    act.wait_ge(*due("gu", 2))
                    split_panel()
                act.wait_ge(*due("ff", 2))
                ff_halves(4)
                for n in range(2, down_panels):
                    act.wait_ge(*due("half_used"))
                    split_panel()
                    ff_halves(4 * n)
                due("half_used", 2)

            def ff_halves(k0):
                for k in range(k0, min(k0 + 4, FB)):
                    to("hi", f(rounded(ff_high(k)), proj[:, k, :], ACT.Copy))

            def project_even():
                n_c = 0
                for m in range(23):
                    width = P if m < 22 else 16
                    act.wait_ge(*due("lin"))
                    to("proj", f(proj[0:width, m, :], ps[0:width, m % 4, :], ACT.Copy))
                    if m in CTX_BLOCKS:
                        act.wait_ge(*due("lin_c"))
                        to("proj_c", f(ctx_proj(n_c)[0:width, :], ps[0:width, 4 + n_c % 4, 0:TC], ACT.Copy))
                        n_c += 1

            def attention():
                for i in range(4):
                    act.wait_ge(*due("krep"))
                    g, c = i // 2, i % 2
                    dst = e_krep[:, g, 0:TC] if c else e_krep[:, g, TC:TC + T]
                    to("krep_sb", f(dst, ps[:, 2 * c + g, 0:TC if c else T], ACT.Copy))
                act.wait_ge(*due("vt"))
                link(f(e_vtok[:, 0:4, :], ps[:, 4, :].rearrange("p (j f) -> p j f", j=4), ACT.Copy))
                to("vt_sb", f(e_vtok[:, 4:6, :], ps[:, 5, 0:256].rearrange("p (j f) -> p j f", j=2), ACT.Copy))

                def exponentials(i):
                    o = 4 * (i % 4)
                    act.wait_ge(*due("smax"))
                    s = ps[:, i % 2 * 2:i % 2 * 2 + 2, :].rearrange("p b k -> p (b k)")[:, 0:768]
                    to("pexp", f(e_prob[:, i % 2, :], s, ACT.Exp, bias=stats[:, o + 1:o + 2], accum_out=stats[:, o + 2:o + 3]))

                def tokens_out(i):
                    hd, n = i // NT, i % NT
                    act.wait_ge(*due("att"))
                    act.wait_ge(*due("recip"))
                    at = 256 + hd // 4 * 64
                    to("mixed", f(e_tok[:, n, hd * 64:hd * 64 + 64], ps[:, 5 + i % 2 * 2, at:at + 64], ACT.Identity,
                                  scale=stats[:, 4 * (i % 4) + 3:4 * (i % 4) + 4]))

                exponentials(0)
                for i in range(8 * NT):
                    if i < 8 * NT - 1:
                        exponentials(i + 1)
                    act.wait_ge(*due("probT"))
                    bank = 4 + i % 2 * 2
                    f(e_probT[:, i % 2, 0:4, :], ps[:, bank, :].rearrange("p (j q) -> p j q", j=4), ACT.Copy)
                    to("probT_sb", f(e_probT[:, i % 2, 4:6, :], ps[:, bank + 1, 0:256].rearrange("p (j q) -> p j q", j=2),
                                     ACT.Copy))
                    if i:
                        tokens_out(i - 1)
                tokens_out(8 * NT - 1)
                features_out()

            def conv_even():
                conditions("even")
                for b in range(12):
                    act.wait_ge(*due("conv"))
                    t = T if b < 8 else TC
                    to("conv_exp", f(rope_b[:, b % 2, 0:t], rope_a[:, b % 2, 0:t], ACT.Exp, scale=-1.0))
                    if b < len(PLANS["even"]):
                        mod_row(b)
                due("mod_tr", 2)

            def mlstm():
                act.wait_ge(*due("m_gates"))
                to("m_raw", f(m_raw, ps[:, 7, 0:96], ACT.Copy))
                for what in range(2):
                    for j in range(6):
                        act.wait_ge(*due("m_tok"))
                        to("m_tok_sb", f((m_kt if what else m_vt)[:, j, :], ps[:, j % 4 if what == 0 else (j + 2) % 4, :], ACT.Copy))
                act.wait_ge(*due("m_sp"))
                link(f(m_b, m_lf, ACT.Abs))
                link(f(m_b, m_b, ACT.Exp, scale=-1.0))
                to("m_ln", f(m_b, m_b, ACT.Ln, bias=1.0))
                act.wait_ge(*due("m_b"))
                link(f(m_b, ps[:, 6, 0:64].rearrange("p (d n) -> p d n", d=2)[:, :, 0:24], ACT.Copy))
                to("m_b_sb", f(m_tot, ps[:, 6, 64:128].rearrange("p (d n) -> p d n", d=2)[:, :, 0:24], ACT.Copy))
                for step in range(6):
                    act.wait_ge(*due("m_cols"))
                    link(f(m_ws, m_ws, ACT.Exp))
                    to("m_ws", f(m_dec, m_dec, ACT.Exp))
                    if step >= 2:
                        link(f(m_wi, m_wi, ACT.Exp))
                        link(f(m_floor, m_floor, ACT.Exp, scale=-1.0))
                        act.wait_ge(*due("m_log"))
                        to("m_exp", f(m_wt_raw, m_wt_raw, ACT.Exp))
                        act.wait_ge(*due("m_wT"))
                        to("m_wT_sb", f(m_wT, ps[:, 0:2, :].rearrange("p b (i t) -> p (b i) t", i=4), ACT.Copy))
                act.wait_ge(*due("m_ss"))
                link(f(stats[:, 16:32], stats[:, 0:16], ACT.Ln, scale=1.0 / P, bias=EPS))
                to("m_rs", f(stats[:, 16:32], stats[:, 16:32], ACT.Exp, scale=-0.5))
                to("gate_exp", f(proj[:, 18:22, :], proj[:, 18:22, :], ACT.Exp, scale=-1.0))

            def experts():
                act.wait_ge(*due("r_sub"))
                to("r_exp", f(r_aff, r_aff, ACT.Exp))
                for i in range(8):
                    n, half = i // 2, i % 2
                    act.wait_ge(*due("r_tok"))
                    to("r_tok_sb", f(h_tok[:, n, half * 512:half * 512 + 512], ps[:, 4 + half, :], ACT.Copy))
                act.wait_ge(*due("r_affT"))
                to("r_affT_sb", f(r_affT[0:E, 0, :], ps[0:E, 1, :], ACT.Copy))
                act.wait_ge(*due("r_thr_rows"))
                to("r_thr_sb", f(r_thr, ps[:, 2, 0:E], ACT.Copy))

                def selected():
                    act.wait_ge(*due("x_sel"))
                    to("x_sel_sb", f(x_sel, ps[:, 6:8, :].rearrange("p b (i c) -> p (b i) c", i=4), ACT.Copy))

                selected()
                for p in range(8):
                    act.wait_ge(*due("e_gate"))
                    to("e_exp", f(e_tmp, ps[:, 0:2, :].rearrange("p b f -> p (b f)"), ACT.Exp, scale=-1.0))
                    for n in gate_tiles.get(p, ()):
                        act.wait_ge(*due("r_pgT"))
                        to("r_pgT_sb", f(r_pgT[:, :, n * P:n * P + P],
                                         ps[:, 6:8, :].rearrange("p b (i t) -> p (b i) t", i=4), ACT.Copy))
                    if p < 7:
                        selected()
                    act.wait_ge(*due("aT"))
                    to("aT_sb", f(e_actT, ps[:, 0:2, :].rearrange("p b (i c) -> p (b i) c", i=4), ACT.Copy))
                    act.wait_ge(*due("e_down"))
                    to("y_sb", f(y_store[:, p, :], ps[:, 4:6, :].rearrange("p b f -> p (b f)"), ACT.Copy))

            def layer(l):
                if l:
                    act.dma_start(positions, a["positions"].partition_broadcast(P)).then_inc(sem["pos_in"], 16)
                split_panel()
                norm(x, h, coef[:, 0, :], mod[:, 0, 0, :], mix)
                split_panel()
                project_halved(22, proj, 8)

                barrier()
                trig()
                head_norm(proj[:, 0:5, :], True)
                barrier()
                windows(l)
                barrier()
                hgrn()
                barrier()
                conditions(f"layer{l}")
                gate_exp(proj[:, 12:14, :])
                head_norm(mix[:, 4:6, :], True)
                conv_silu(6)
                barrier()
                head_norm(proj[:, 14:18, :], False)
                barrier()
                delta(l)
                barrier()
                gate_exp(proj[:, 20:22, :])
                head_norm(mix[:, 6:8, :], True)
                barrier()
                split_mix()
                barrier()
                split_panel()
                norm(x, h, coef[:, 1, :], mod[:, 0, 3, :], mix)
                split_panel()
                swiglu()
                barrier()

            act.dma_start(stage_tables[:, 0:first_t["band0"][1]], a["first"]).then_inc(sem["const_in"], 16)
            act.dma_start(positions, a["positions"].partition_broadcast(P)).then_inc(sem["const_in"], 16)
            act.wait_ge(sem["const_in"], 64)
            act.wait_ge(*due("lb"))
            to("lb_exp", f(stats[:, 232:234], stats[:, 232:234], ACT.Exp))
            conditions("start")
            for i in range(2):
                mod_row(i)
            due("mod_tr", 2)
            barrier()
            for l in range(2):
                layer(l)

            def moe_layer(w):
                barrier()
                norm(x, h, coef[:, 1, :], mod[:, w, 3, :])
                barrier()
                experts()
                barrier()

            act.dma_start(x_ctx, a["ctxT"].rearrange("(k p) t -> p k t", p=P)).then_inc(sem["ctx_in"], 16)
            act.dma_start(stage_tables[:, 0:even_t["mask_b"][1]], a["even"]).then_inc(sem["ctx_in"], 16)
            norm(x, h, coef[:, 0, :], mod[:, 0, 0, :])
            barrier()
            act.wait_ge(*due("ctx_in", 32))
            norm(x_ctx, h_ctx, coef[:, 2, :], mod[:, 1, 0, :])
            barrier()
            project_even()
            barrier()
            head_norm(proj[:, 0:5, :], True)
            barrier()
            head_norm(ctx_proj(0).unsqueeze(1), True)
            barrier()
            attention()
            barrier()
            conv_even()
            barrier()
            mlstm()
            barrier()
            split_mix()
            moe_layer(0)
            act.dma_start(stage_tables[:, :], a["pool"]).then_inc(sem["pool_in"], 16)
            barrier()
            split_panel()
            norm(x, h, coef[:, 0, :], mod[:, 1, 0, :], mix)
            split_panel()
            project_halved(8, proj)
            barrier()
            moe_layer(1)
            norm(x, h, param("final"), None)
            act.wait_ge(*due("h", 0))
            act.dma_start(out.rearrange("(k p) t -> p k t", p=P), h).then_inc(sem["stored"], 16)
            act.wait_ge(sem["stored"], 16)

        @block.vector
        def _(dve):
            due = Due(sem)
            link = make_link(dve, "dve_step")
            tt, ts, stt = dve.tensor_tensor, dve.tensor_scalar, dve.scalar_tensor_tensor

            def to(signal, ins):
                ins.then_inc(sem[signal], 1)

            def barrier():
                dve.drain().then_inc(sem["stage"], 1)
                dve.wait_ge(*due("stage", 3))

            def inverse_of_one_plus(v):
                link(ts(v, v, 1.0, None, ALU.add))
                link(dve.reciprocal(v, v))

            def conditions(name):
                dve.wait_ge(*due("cond_exp"))
                groups = CONDITIONS[name]
                inverse_of_one_plus(cond[:, 0:len(sum(groups, ())), :])
                at = 0
                for g, cols in enumerate(groups):
                    for w, col in enumerate(cols):
                        link(tt(cond[:, at, :], cond[:, at, :], param(col), ALU.mult))
                        i = dve.tensor_copy(creps[g][:, :, 32 * w // len(cols):32 * (w + 1) // len(cols)],
                                            cond[:, at, :].unsqueeze(2).to_broadcast([P, KB, 32 // len(cols)]))
                        at += 1
                to("cond", i)

            def mod_column(plan, n):
                vec = plan[n]
                dve.wait_ge(*due("mod_tr"))
                turned = ps[:, 2 + n % 2, 0:256].rearrange("p (j r) -> p j r", j=2)
                for w, dst in enumerate(vec.to):
                    for g in range(4):
                        i = tt(mod[:, dst, vec.v, 2 * g:2 * g + 2], turned[:, :, 32 * g + 16 * w],
                               param(vec.bias)[:, vec.v * KB + 2 * g:vec.v * KB + 2 * g + 2], ALU.add)
                to("mod_ready", i)
                if n == len(plan) - 1:
                    dve.wait_ge(*due("mod_ready", len(plan)))

            def coefficient(w, gain, v, cond_=0):
                link(stt(out=coef[:, w, :], in0=mod[:, cond_, v, :], scalar=1.0, in1=gain, op0=ALU.add, op1=ALU.mult))

            splits = [0]

            def lower(hi, v):
                dve.wait_ge(*due("hi"))
                to("lo", tt(rounded(v), v, rounded(hi), ALU.subtract))

            def lower_panels(n=1):
                for _ in range(n):
                    lower(panel_high(splits[0]), slot(halved[splits[0]]))
                    splits[0] += 1

            def norm(x_, h_, hi=None):
                t = x_.shape[2]
                dve.wait_ge(*due("rstd"))
                for k in range(KB):
                    to("xn", tt(h_[:, k, :], x_[:, k, :], rstd[:, 0, 0:t], ALU.mult))
                    if hi is not None and k >= 2:
                        lower(hi[:, k - 2, :], h_[:, k - 2, :])
                if hi is not None:
                    for k in (KB - 2, KB - 1):
                        lower(hi[:, k, :], h_[:, k, :])

            def rope_tables(l):
                a_, k_ = rope_a[:, 0, :], rope_a[:, 1, :]
                if l:
                    dve.wait_ge(*due("pos_in", 16))
                two_pi = float(2 * np.pi)
                c1 = 6.28125
                c2 = float(np.float32(two_pi - c1))
                c3 = float(np.float32(two_pi - c1 - c2))
                magic = 1.5 * 2.0 ** 23
                link(ts(a_, positions, const("freq"), None, ALU.mult))
                link(ts(k_, a_, 1.0 / two_pi, magic, ALU.mult, ALU.add))
                link(ts(k_, k_, magic, None, ALU.subtract))
                for c in (c1, c2, c3):
                    link(stt(out=a_, in0=k_, scalar=-c, in1=a_, op0=ALU.mult, op1=ALU.add))
                link(ts(a_, a_, 3.1415925, -3.1415925, ALU.min, ALU.max))
                to("trig", ts(k_, a_, 0.5, None, ALU.mult))
                dve.wait_ge(*due("trig_sb"))
                link(tt(cos_t, cos_t, cos_t, ALU.mult))
                link(ts(cos_t, cos_t, -2.0, 1.0, ALU.mult, ALU.add))

            def rope(gains, cos_, sin_):
                n = len(gains)
                for b in range(n):
                    dve.wait_ge(*due("gn_rstd"))
                    to("gn", stt(out=proj[:, b, :], in0=proj[:, b, :], scalar=gains[b], in1=gn_rstd[:, b % 2, :],
                                 op0=ALU.mult, op1=ALU.mult))
                    due("gn")
                    dve.wait_ge(*due("rot"))
                    link(tt(rope_b[:, 0, :], ps[:, 6 + b % 2, :], sin_, ALU.mult))
                    link(tt(proj[:, b, :], proj[:, b, :], cos_, ALU.mult))
                    to("roped", tt(proj[:, b, :], proj[:, b, :], rope_b[:, 0, :], ALU.add))
                    dve.wait_ge(*due("roped"))

            def windows(l):
                to("krep_pad", dve.memset(krep[:, :, 0:P], 0.0))

                def maxima(hd):
                    pr, o = prob[:, hd % 2, :, :], 24 * (hd % 2)
                    dve.wait_ge(*due("score"))
                    s = ps[:, hd % 2 * 2:hd % 2 * 2 + 2, :].rearrange("p b (j k) -> p (b j) k", j=2)
                    tt(pr[:, 0:1, :], s[:, 0:1, :], table(first_t, "band0").unsqueeze(1), ALU.add)
                    link(tt(pr[:, 1:4, :], s[:, 1:4, :], table(first_t, "band").unsqueeze(1).to_broadcast([P, 3, 256]),
                            ALU.add))
                    link(dve.tensor_reduce(stats[:, o:o + 4], pr, AX.X, ALU.max))
                    to("smax", ts(stats[:, o + 4:o + 8], stats[:, o:o + 4], param(f"sinks{l}", hd), -1.0, ALU.max, ALU.mult))

                def normalise(hd):
                    o = 24 * (hd % 2)
                    dve.wait_ge(*due("w_att"))
                    to("w_mixed", tt(w_tok[:, :, hd * 64:hd * 64 + 64], ps[:, 6 + hd % 2, 0:256].rearrange("p (n e) -> p n e", n=4),
                                     stats[:, o + 16:o + 20].unsqueeze(2).to_broadcast([P, 4, 64]), ALU.mult))

                maxima(0)
                for hd in range(8):
                    if hd < 7:
                        if hd >= 1:
                            dve.wait_ge(*due("probT"))
                        maxima(hd + 1)
                    if hd:
                        normalise(hd - 1)
                    o = 24 * (hd % 2)
                    dve.wait_ge(*due("pexp"))
                    link(tt(stats[:, o + 16:o + 20], stats[:, o + 8:o + 12], stats[:, o + 12:o + 16], ALU.add))
                    link(dve.reciprocal(stats[:, o + 16:o + 20], stats[:, o + 16:o + 20]))
                normalise(7)
                due("probT", 2)

            def gated_out(at, gain, gate):
                s = two(work, 3072)
                dve.wait_ge(*due("gate_exp"))
                inverse_of_one_plus(s)
                link(tt(s, s, gate, ALU.mult))
                for b in range(2):
                    m = mix[:, at + b, :]
                    dve.wait_ge(*due("gn_rstd"))
                    to("gn", stt(out=m, in0=m, scalar=gain, in1=gn_rstd[:, b, :], op0=ALU.mult, op1=ALU.mult))
                    dve.wait_ge(*due("gn"))
                    link(tt(m, m, s[:, b, :], ALU.mult))

            def lower_bounds():
                lb, rest = stats[:, 232:234], stats[:, 236:238]
                link(tt(lb, param("lb0"), param("lb1"), ALU.subtract))
                to("lb", ts(lb, lb, 60.0, -60.0, ALU.min, ALU.max))
                dve.wait_ge(*due("lb_exp"))
                inverse_of_one_plus(lb)
                link(ts(rest, lb, -1.0, 1.0, ALU.mult, ALU.add))

            def hgrn(l):
                z, q = proj[:, 8:10, :], proj[:, 6:8, :]
                to("b_z", ts(z, z, -80.0, None, ALU.max))
                dve.wait_ge(*due("b_ez"))
                inverse_of_one_plus(z)
                for b in range(2):
                    if l:
                        link(ts(z[:, b, :], z[:, b, :], stats[:, 236 + b:237 + b], stats[:, 232 + b:233 + b],
                                ALU.mult, ALU.add))
                to("b_f", ts(z, z, 2.0 ** -64, None, ALU.max))
                dve.wait_ge(*due("b_lf"))
                link(ts(z, z, -1.0, 1.0, ALU.mult, ALU.add))
                for b in range(2):
                    link(dve.tensor_tensor_scan(b_cum[:, b, :], table(first_t, "resets"), b_d[:, b, :], 0.0,
                                                ALU.mult, ALU.add))
                to("b_qk", dve.memset(stats[:, 60:61], 0.0))

                def blocks_of(v, n):
                    return v.rearrange("p b (j t) -> p (b j) t", t=n)

                def difference(s):
                    c = blocks_of(b_cum, 2 * s)
                    to("b_diff", tt(blocks_of(b_d, 2 * s), c, c[:, :, s - 1:s].to_broadcast([P, T // s, 2 * s]), ALU.subtract))

                def gather(n):
                    name, bank = f"level{LEVELS[n - 1]}" if n else None, n % 2 * 4
                    for hd in range(H1):
                        dve.wait_ge(*due("b_score"))
                        s = ps[:, bank + hd, :].rearrange("p (c t) -> p c t", c=4)
                        o = b_at[:, hd, :].rearrange("p (c t) -> p c t", c=4)
                        if name is None:
                            to("b_acc", tt(o, s, ident.unsqueeze(1).to_broadcast([P, 4, P]), ALU.mult))
                        else:
                            m = table(first_t, name).bitcast(I32).unsqueeze(1).to_broadcast([P, 4, P])
                            to("b_acc", dve.copy_predicated(o, m, s))
                    dve.wait_ge(*due("b_acc", H1))

                difference(LEVELS[0])
                for n in range(1, len(LEVELS) + 1):
                    dve.wait_ge(*due("b_decay"))
                    tt(b_q[n % 2], q, b_e, ALU.mult)
                    to("b_qk", tt(b_k[n % 2], z, b_e, ALU.mult))
                    dve.wait_ge(*due("b_qk", 2 if n == 1 else 1))
                    if n < len(LEVELS):
                        difference(LEVELS[n])
                    gather(n - 1)
                gather(len(LEVELS))
                c = blocks_of(b_cum, P)
                to("b_qd", tt(blocks_of(b_d, P), c, c[:, :, P - 1:P].to_broadcast([P, 8, P]), ALU.subtract))
                dve.wait_ge(*due("b_decay"))
                link(tt(b_e, q, b_e, ALU.mult))
                to("b_kd", tt(b_d, z, b_d, ALU.mult))
                to("b_state", dve.memset(b_s, 0.0))
                for c in range(NT - 1):
                    dve.wait_ge(*due("b_ds"))
                    link(tt(b_tmp, ps[:, 4, 0:256].rearrange("p (b e) -> p b e", b=2),
                            halves.unsqueeze(1).to_broadcast([P, 2, P]), ALU.mult))
                    for b in range(2):
                        i = stt(out=b_s[:, b, :], in0=b_s[:, b, :], scalar=stats[:, 32 + 4 * b + c:33 + 4 * b + c],
                                in1=b_tmp[:, b, :], op0=ALU.mult, op1=ALU.add)
                    to("b_state", i)
                    due("b_state")
                due("b_state")

            def convolve(l):
                plan = PLANS[f"layer{l}"]
                for b in range(6):
                    src, dst = proj[:, 14 + b, :], rope_a[:, b % 2, :]
                    w = [param(f"conv{l}", j * 6 + b) for j in range(4)]
                    link(ts(dst, src, w[3], None, ALU.mult))
                    for back in range(1, 4):
                        i = stt(out=dst[:, back:T], in0=src[:, 0:T - back], scalar=w[3 - back], in1=dst[:, back:T],
                                op0=ALU.mult, op1=ALU.add)
                        if back < 3:
                            link(i)
                    to("conv", i)
                    dve.wait_ge(*due("conv_exp"))
                    inverse_of_one_plus(rope_b[:, b % 2, :])
                    to("conv_done", tt(src, dst, rope_b[:, b % 2, :], ALU.mult))
                    dve.wait_ge(*due("conv_done"))
                    if b:
                        mod_column(plan, b - 1)
                mod_column(plan, 5)
                coefficient(1, param(f"norm_ffn{l}"), 4)
                if l == 0:
                    coefficient(0, param("norm_mix1"), 1)
                else:
                    coefficient(0, param("norm10"), 1)
                    coefficient(2, param("norm10"), 1, 1)

            def l2(scales):
                for b, s in enumerate(scales):
                    m = proj[:, 14 + b, :]
                    dve.wait_ge(*due("gn_rstd"))
                    to("gn", stt(out=m, in0=m, scalar=s, in1=gn_rstd[:, b % 2, :], op0=ALU.mult, op1=ALU.mult))
                due("gn", len(scales) - 1)
                dve.wait_ge(*due("gn"))

            def by16(v):
                return v.rearrange("p h (c t) -> p (h c) t", c=4)

            def delta(l):
                sp = g_sp[:, 0:32].rearrange("p (c g h) -> p c g h", c=4, g=2)

                def hc(v):
                    return v.rearrange("p (h c) -> p h c", c=4)

                dve.wait_ge(*due("g_gates_sb"))
                inverse_of_one_plus(g_beta)
                link(ts(stats[:, 40:44], stats[:, 40:44], -1.0, None, ALU.mult))
                to("g_sum", tt(hc(g_g), sp[:, :, 1, :].rearrange("p c h -> p h c"),
                               param(f"dt{l}").unsqueeze(2).to_broadcast([P, 4, 4]), ALU.add))
                dve.wait_ge(*due("g_sum"))
                dve.wait_ge(*due("g_ln"))
                link(stt(out=g_g, in0=g_g, scalar=0.0, in1=g_kdf, op0=ALU.max, op1=ALU.add))
                to("g_g", tt(hc(g_g), hc(g_g), stats[:, 40:44].unsqueeze(2).to_broadcast([P, 4, 4]), ALU.mult))
                dve.wait_ge(*due("g_v_raw"))
                for c in range(NT):
                    v = g_vt[:, c, :].rearrange("p (h e) -> p h e", h=4)
                    i = tt(v, v, hc(g_beta)[:, :, c:c + 1].to_broadcast([P, 4, 64]), ALU.mult)
                link(i)
                dve.wait_ge(*due("g_cols"))
                for hd in range(H1):
                    dve.wait_ge(*due("g_rows"))
                    dve.wait_ge(*due("g_eg"))
                    s = ps[:, hd, :].rearrange("p (c t) -> p c t", c=4)
                    to("g_diffs", tt(g_L[:, hd, :].rearrange("p (c t) -> p c t", c=4), s,
                                     hc(g_gt)[:, hd, :].unsqueeze(2).to_broadcast([P, 4, P]), ALU.subtract))
                dve.wait_ge(*due("g_diffs", H1))
                to("g_diff", ts(g_L, g_L, 0.0, None, ALU.min))
                to("g_kdiff", tt(g_kdf, g_tot, g_gt, ALU.subtract))
                for hd in range(H1):
                    r = slice(hd % 2 * 64, hd % 2 * 64 + 64)
                    dve.wait_ge(*due("g_brows"))
                    i = tt(g_kb[r, hd // 2, :], proj[r, 16 + hd // 2, :], ps[r, hd, :], ALU.mult)
                to("g_kb", i)
                dve.wait_ge(*due("g_kb"))
                dve.wait_ge(*due("g_decay"))
                for dst in (g_A, g_qk):
                    for hd in range(H1):
                        dve.wait_ge(*due("g_score"))
                        to("g_acc", tt(dst[:, hd, :], ps[:, hd, :], g_L[:, hd, :], ALU.mult))
                dve.wait_ge(*due("g_acc", 2 * H1))
                levels = tuple(reversed(LEVELS[:-1]))

                def level_blocks(n):
                    m = table(first_t, f"level{levels[n]}").unsqueeze(1).to_broadcast([P, 8, P])
                    for half in range(2):
                        v = slice(2 * half, 2 * half + 2)
                        to("g_al", tt(by16(g_al[n % 2][:, v, :]), by16(g_A[:, v, :]), m, ALU.mult))

                link(tt(by16(g_A), by16(g_A), const("below").unsqueeze(1).to_broadcast([P, 16, P]), ALU.mult))
                link(tt(by16(g_Y), by16(g_A), table(first_t, "level1").unsqueeze(1).to_broadcast([P, 16, P]), ALU.mult))
                to("g_y", tt(by16(g_Y), ident.unsqueeze(1).to_broadcast([P, 16, P]), by16(g_Y), ALU.subtract))
                q = proj[:, 14:16, :]
                link(tt(g_kb, g_kb, g_eg, ALU.mult))
                link(tt(q, q, g_eg, ALU.mult))
                level_blocks(0)
                link(tt(by16(g_qk), by16(g_qk), const("upto").unsqueeze(1).to_broadcast([P, 16, P]), ALU.mult))
                dve.wait_ge(*due("g_kdf"))
                dve.wait_ge(*due("g_k_sb"))
                for c in range(NT):
                    v = g_kdt[:, c, :].rearrange("p (h e) -> p h e", h=4)
                    i = tt(v, v, hc(g_kdf)[:, :, c:c + 1].to_broadcast([P, 4, 64]), ALU.mult)
                link(i)
                dve.wait_ge(*due("g_t_sb", H1))
                for n, s in enumerate(levels):
                    if n:
                        dve.wait_ge(*due("g_x", H1))
                    if n + 1 < len(levels):
                        level_blocks(n + 1)
                    for hd in range(H1):
                        dve.wait_ge(*due("g_dy"))
                        if s != LEVELS[0]:
                            dve.wait_ge(*due("g_dt"))
                            to("g_tt", tt(g_T[:, hd, :], g_T[:, hd, :], ps[:, 6 + hd % 2, :], ALU.subtract))
                        to("g_yt", tt(g_Y[:, hd, :], g_Y[:, hd, :], ps[:, 4 + hd % 2, :], ALU.subtract))
                due("g_x", H1)
                dve.wait_ge(*due("g_yt", H1 * len(LEVELS[:-1])))
                to("g_state", dve.memset(g_s, 0.0))
                for c in range(NT):
                    dve.wait_ge(*due("g_r"))
                    to("g_rhs", tt(g_rhs, g_vt[:, c, :], ps[:, 0, 0:256], ALU.subtract))
                    dve.wait_ge(*due("g_ds"))
                    if c < NT - 1:
                        dve.wait_ge(*due("g_state"))
                        link(tt(g_stmp, ps[:, 4, 0:256].rearrange("p (b e) -> p b e", b=2),
                                halves.unsqueeze(1).to_broadcast([P, 2, P]), ALU.mult))
                        for b in range(2):
                            i = stt(out=g_s[:, b, :], in0=g_s[:, b, :], scalar=g_last[:, 4 * b + c:4 * b + c + 1],
                                    in1=g_stmp[:, b, :], op0=ALU.mult, op1=ALU.add)
                        to("g_state", i)
                due("g_state")

            def residual(gate, signal, done, blocks=range(KB)):
                for m in blocks:
                    add(gate, m, m % 4 if signal == "y" else m, signal, done)

            def project_out(gate):
                lower_panels()
                for k in range(KB):
                    lower(h[:, k, :], mix[:, k, :])
                lower_panels()
                for n in range(4):
                    if n < 2:
                        lower_panels()
                    residual(gate, "y", "y_used", range(2 * n, 2 * n + 2))

            def add(gate, m, bank, signal, done):
                dve.wait_ge(*due(signal))
                to(done, stt(out=x[:, m, :], in0=ps[:, bank, :], scalar=gate[:, m:m + 1], in1=x[:, m, :],
                             op0=ALU.mult, op1=ALU.add))

            def ff_halves(k0):
                for k in range(k0, min(k0 + 4, FB)):
                    lower(ff_high(k), proj[:, k, :])

            def swiglu(gate):
                for jj in range(FB // 2):
                    for j in range(2):
                        e = rope_a[:, j, :]
                        dve.wait_ge(*due("ff_exp"))
                        inverse_of_one_plus(e)
                        link(tt(e, ps[:, jj % 2 * 4 + j, :], e, ALU.mult))
                    lower_panels()
                    if jj == FB // 2 - 1:
                        ff_halves(0)
                    dve.wait_ge(*due("gu", 4))
                    for j in range(2):
                        to("ff", tt(proj[:, 2 * jj + j, :], ps[:, jj % 2 * 4 + 2 + j, :], rope_a[:, j, :], ALU.mult))
                    lower_panels()
                ff_halves(4)
                for n in range(2, down_panels):
                    lower_panels()
                    ff_halves(4 * n)
                    if n == down_panels // 2 + 1:
                        for m in range(4):
                            add(gate, m, 4 + m, "down", "down_x")
                for m in range(4, KB):
                    add(gate, m, m - 4, "down", "down_x")

            def head_norm_ctx():
                m = ctx_proj(0)
                dve.wait_ge(*due("gn_rstd"))
                to("gn", stt(out=m, in0=m, scalar=param("gk"), in1=gn_rstd[:, 0, 0:TC], op0=ALU.mult, op1=ALU.mult))
                due("gn")

            def attention():
                def maxima(i):
                    o = 4 * (i % 4)
                    dve.wait_ge(*due("score"))
                    s = ps[:, i % 2 * 2:i % 2 * 2 + 2, :].rearrange("p b k -> p (b k)")[:, 0:768]
                    link(dve.tensor_reduce(stats[:, o:o + 1], s, AX.X, ALU.max))
                    to("smax", ts(stats[:, o + 1:o + 2], stats[:, o:o + 1], -1.0, None, ALU.mult))

                maxima(0)
                for i in range(8 * NT):
                    if i < 8 * NT - 1:
                        if i >= 1:
                            dve.wait_ge(*due("probT"))
                        maxima(i + 1)
                    o = 4 * (i % 4)
                    dve.wait_ge(*due("pexp"))
                    to("recip", dve.reciprocal(stats[:, o + 3:o + 4], stats[:, o + 2:o + 3]))
                due("probT", 2)

            def conv_even():
                plan = PLANS["even"]
                conditions("even")
                for b in range(12):
                    full = b if b < 8 else b - 4
                    t = T if b < 8 else TC
                    src = proj[:, 6 + b, :] if b < 8 else ctx_proj(2 + b - 8)
                    dst = rope_a[:, b % 2, 0:t]
                    w = [param("conv_e", j * 8 + full) for j in range(3)]
                    link(ts(dst, src, w[1], None, ALU.mult))
                    link(stt(out=dst[:, 1:t], in0=src[:, 0:t - 1], scalar=w[0], in1=dst[:, 1:t], op0=ALU.mult, op1=ALU.add))
                    to("conv", stt(out=dst[:, 0:t - 1], in0=src[:, 1:t], scalar=w[2], in1=dst[:, 0:t - 1],
                                   op0=ALU.mult, op1=ALU.add))
                    dve.wait_ge(*due("conv_exp"))
                    inverse_of_one_plus(rope_b[:, b % 2, 0:t])
                    if full < 4:
                        link(tt(src, dst, rope_b[:, b % 2, 0:t], ALU.mult))
                    else:
                        link(stt(out=src, in0=dst, scalar=float(np.float32(P ** -0.5)), in1=rope_b[:, b % 2, 0:t],
                                 op0=ALU.mult, op1=ALU.mult))
                    if 0 < b <= len(plan):
                        mod_column(plan, b - 1)
                coefficient(1, param("norm20"), 4)

            def mlstm():
                dve.wait_ge(*due("m_raw"))
                raw = m_raw.rearrange("p (j d g h) -> p j d g h", j=6, d=2, g=2)
                bias = param("b_gate").rearrange("p (d g h) -> p d g h", d=2, g=2)
                for d in range(2):
                    for g, dst in ((0, m_ig), (1, m_lf)):
                        i = tt(dst[:, d, :].rearrange("p (j h) -> p j h", j=6), raw[:, :, d, g, :],
                               bias[:, d:d + 1, g, :].to_broadcast([P, 6, 4]), ALU.add)
                to("m_sp", i)
                dve.wait_ge(*due("m_ln"))
                to("m_lf", stt(out=m_lf, in0=m_lf, scalar=0.0, in1=m_b, op0=ALU.min, op1=ALU.subtract))
                dve.wait_ge(*due("m_b_sb"))
                to("m_a", tt(m_a, m_ig, m_b, ALU.subtract))
                link(dve.memset(m_z, 0.0))
                link(dve.memset(m_n, 0.0))
                link(dve.memset(m_prev, NEG))
                link(dve.memset(m_h, 0.0))
                dve.wait_ge(*due("m_tok_sb", 12))
                dve.wait_ge(*due("m_a"))

                def both(v, tiles):
                    return [v[:, d, 4 * tiles[d]:4 * tiles[d] + 4] for d in range(2)]

                def eight(v):
                    return v.unsqueeze(2).to_broadcast([P, 8, P])

                for step in range(6):
                    tiles = (step, M_BACK[step])
                    dve.wait_ge(*due("m_rows"))
                    rows_ = ps[:, 0:2, :].rearrange("p b (i s) -> p (b i) s", i=4)
                    link(dve.tensor_reduce(m_am, rows_, AX.X, ALU.max))
                    if step >= 2:
                        for d, name in enumerate(("mask_f", "mask_b")):
                            i = tt(m_wt_raw[:, 4 * d:4 * d + 4, :], rows_[:, 4 * d:4 * d + 4, :],
                                   table(even_t, name).unsqueeze(1).to_broadcast([P, 4, P]), ALU.add)
                        link(i)
                        link(dve.tensor_reduce(m_rm, m_wt_raw, AX.X, ALU.max))
                        link(tt(m_M, m_rm, m_prev, ALU.max))
                        link(tt(m_wi, m_prev, m_M, ALU.subtract))
                        for d in range(2):
                            i = tt(m_floor[:, 4 * d:4 * d + 4], both(m_b, tiles)[d], m_M[:, 4 * d:4 * d + 4], ALU.add)
                        link(i)
                    link(tt(m_end, m_am, m_prev, ALU.max))
                    link(tt(m_dec, m_prev, m_end, ALU.subtract))
                    for d in range(2):
                        s = slice(4 * d, 4 * d + 4)
                        tt(m_ws[:, s], both(m_a, tiles)[d], m_end[:, s], ALU.subtract)
                        i = tt(m_prev[:, s], both(m_tot, tiles)[d], m_end[:, s], ALU.add)
                    to("m_cols", i)
                    if step >= 2:
                        to("m_log", tt(m_wt_raw, m_wt_raw, eight(m_M), ALU.subtract))
                        dve.wait_ge(*due("m_exp"))
                        dve.wait_ge(*due("m_qk"))
                        link(tt(m_wt_raw, m_wt_raw, ps[:, 2:4, :].rearrange("p b (i s) -> p (b i) s", i=4), ALU.mult))
                        to("m_w", dve.tensor_reduce(m_rs, m_wt_raw, AX.X, ALU.add))
                    if step < 5:
                        dve.wait_ge(*due("m_ws"))
                        for d in range(2):
                            s = slice(4 * d, 4 * d + 4)
                            i = tt(m_kw[:, s, :], m_kt[:, tiles[d], :].rearrange("p (h f) -> p h f", h=4),
                                   m_ws[:, s].unsqueeze(2).to_broadcast([P, 4, P]), ALU.mult)
                        to("m_kw", i)
                    else:
                        due("m_ws")
                    if step >= 2:
                        dve.wait_ge(*due("m_inter"))
                        link(tt(m_z, m_z, eight(m_dec), ALU.mult))
                        link(tt(m_tmp, ps[:, 6:8, :].rearrange("p b (i s) -> p (b i) s", i=4), eight(m_wi), ALU.mult))
                        link(tt(m_u, ps[:, 2, 0:8], m_wi, ALU.mult))
                        link(tt(m_u, m_u, m_rs, ALU.add))
                        link(stt(out=m_v, in0=m_u, scalar=-1.0, in1=m_u, op0=ALU.mult, op1=ALU.max))
                        link(tt(m_v, m_v, m_floor, ALU.max))
                        link(dve.reciprocal(m_v, m_v))
                        dve.wait_ge(*due("m_num"))
                        link(tt(m_tmp, m_tmp, ps[:, 4:6, :].rearrange("p b (i s) -> p (b i) s", i=4), ALU.add))
                    else:
                        link(tt(m_z, m_z, eight(m_dec), ALU.mult))
                    if step < 5:
                        link(tt(m_n, m_n, m_dec, ALU.mult))
                        dve.wait_ge(*due("m_ds"))
                        link(tt(m_z, m_z, ps[:, 0:2, :].rearrange("p b (i s) -> p (b i) s", i=4), ALU.add))
                        to("m_state", tt(m_n, m_n, ps[:, 3, 0:8], ALU.add))
                    if step >= 2:
                        link(tt(m_tmp, m_tmp, eight(m_v), ALU.mult))
                        for d in range(2):
                            o = m_h[:, tiles[d] - 2, :].rearrange("p (h e) -> p h e", h=4)
                            link(tt(o, o, m_tmp[:, 4 * d:4 * d + 4, :], ALU.add))
                sqr = cut(proj_all, 0, 2048, j=4, f=T)
                link(tt(sqr, m_h, m_h, ALU.mult))
                to("m_ss", dve.tensor_reduce(stats[:, 0:16], sqr.rearrange("p j (h e) -> p (j h) e", h=4), AX.X, ALU.add))
                dve.wait_ge(*due("m_rs"))
                hs = m_h.rearrange("p j (h e) -> p (j h) e", h=4)
                to("m_h", tt(hs, hs, stats[:, 16:32].unsqueeze(2).to_broadcast([P, 16, P]), ALU.mult))
                dve.wait_ge(*due("gate_exp"))
                g = proj[:, 18:22, :]
                inverse_of_one_plus(g)
                for hd in range(4):
                    dve.wait_ge(*due("m_hT"))
                    i = stt(out=mix[:, 4 + hd, :], in0=ps[:, hd, :], scalar=param("hnorm", hd), in1=g[:, hd, :],
                            op0=ALU.mult, op1=ALU.mult)
                link(i)

            def experts(gate):
                logits = ps[:, 0, 0:64].rearrange("p (n e) -> p n e", n=4)

                def rows16(v):
                    return v.unsqueeze(2).to_broadcast([P, 4, E])

                dve.wait_ge(*due("r_logits"))
                link(dve.tensor_reduce(r_max, logits, AX.X, ALU.max))
                to("r_sub", tt(r_aff, logits, rows16(r_max), ALU.subtract))
                dve.wait_ge(*due("r_exp"))
                link(dve.tensor_reduce(r_max, r_aff, AX.X, ALU.add))
                link(dve.reciprocal(r_max, r_max))
                to("r_aff", tt(r_aff, r_aff, rows16(r_max), ALU.mult))
                dve.wait_ge(*due("r_aff"))
                dve.wait_ge(*due("r_affT_sb"))
                for i in range(CAP // 8):
                    src, dst = r_affT[0:E, i % 2, :], r_affT[0:E, (i + 1) % 2, :]
                    link(dve.max(r_top[0:E, :], src))
                    if i < CAP // 8 - 1:
                        link(dve.match_replace(dst, r_top[0:E, :], src, -1.0))
                to("r_thr", dve.tensor_copy(r_thr_rows[0:E, :], r_top[0:E, 7:8].to_broadcast([E, P])))
                dve.wait_ge(*due("r_thr_sb"))

                def each(v):
                    return v.unsqueeze(1).to_broadcast([P, 4, E])

                link(tt(r_gt, r_aff, each(r_thr), ALU.is_gt))
                to("r_marks", tt(r_eq, r_aff, each(r_thr), ALU.is_equal))
                dve.wait_ge(*due("r_marks"))
                dve.wait_ge(*due("r_count"))
                link(ts(r_need, ps[:, 3, 64:64 + E], -1.0, float(CAP), ALU.mult, ALU.add))
                counts = ps[:, 3, 0:64].rearrange("p (n e) -> p n e", n=4)
                link(tt(r_tmp, counts, each(r_need), ALU.is_le))
                link(tt(r_tmp, r_tmp, r_eq, ALU.mult))
                to("r_marks", tt(r_sel, r_tmp, r_gt, ALU.add))
                dve.wait_ge(*due("r_marks"))
                dve.wait_ge(*due("r_count"))
                link(tt(r_slot, counts, r_sel, ALU.mult))
                link(ts(r_slot, r_slot, 1.0, None, ALU.subtract))
                iota = const("iota").unsqueeze(1).to_broadcast([P, E, CAP])
                for n in range(NT):
                    s = sel[:, n, :].rearrange("p (e c) -> p e c", e=E)
                    i = tt(s, iota, r_slot[:, n, :].unsqueeze(2).to_broadcast([P, E, CAP]), ALU.is_equal)
                to("r_marks", i)
                dve.wait_ge(*due("r_marks"))

                def gated(n):
                    s = sel[:, n, :].rearrange("p (e c) -> p e c", e=E)
                    to("r_pg", tt(r_pg.rearrange("p (e c) -> p e c", e=E), s,
                                  r_aff[:, n, :].unsqueeze(2).to_broadcast([P, E, CAP]), ALU.mult))

                gated(0)
                for p in range(8):
                    for n in gate_tiles.get(p, ()):
                        dve.wait_ge(*due("r_pgT"))
                        if n < NT - 1:
                            gated(n + 1)
                    dve.wait_ge(*due("e_exp"))
                    inverse_of_one_plus(e_tmp)
                    link(tt(e_tmp, e_tmp, ps[:, 0:2, :].rearrange("p b f -> p (b f)"), ALU.mult))
                    if p in combining:
                        for m in combining[p][1]:
                            add(gate, m, 6 + m % 2, "down", "down_x")
                    dve.wait_ge(*due("e_up"))
                    to("e_act", tt(e_act, e_tmp, ps[:, 2:4, :].rearrange("p b f -> p (b f)"), ALU.mult))

            def pooling():
                pad = cut(work, 0, 8 * (T + 2 * PAD), i=8, t=T + 2 * PAD)
                link(dve.memset(pad, 0.0))
                for g, w in enumerate(POOLS):
                    u = proj[:, 2 * g:2 * g + 2, :]
                    s, o = pad[:, 0:2, :], pad[:, 2:4, :]
                    link(dve.tensor_copy(s[:, :, PAD:PAD + T], u))
                    size = 1
                    while size < w:
                        n = T + 2 * PAD - size
                        link(tt(o[:, :, 0:n], s[:, :, 0:n], s[:, :, size:size + n], ALU.add))
                        s, o = o, s
                        size *= 2
                    lo = PAD - w // 2
                    c = table(pool_t, f"count{w}").unsqueeze(1).to_broadcast([P, 2, T])
                    m = proj[:, 8 + 2 * g:10 + 2 * g, :]
                    link(tt(m, s[:, :, lo:lo + T], c, ALU.mult))
                    to("pooled", tt(m, m, u, ALU.subtract))
                    dve.wait_ge(*due("pooled"))
                    if g < 3:
                        link(dve.memset(pad[:, 0:4, :], 0.0))

            def layer(l):
                lower_panels()
                norm(x, h, mix)
                lower_panels(11)
                barrier()
                rope_tables(l)
                link(ts(stats[:, 240:241], param(f"q_norm{l}"), 0.125, None, ALU.mult))
                rope([stats[:, 240:241]] * 4 + [param(f"k_norm{l}")], cos_t, sin_t)
                barrier()
                windows(l)
                barrier()
                hgrn(l)
                barrier()
                conditions(f"layer{l}")
                gated_out(4, param(f"hgrn_norm{l}"), proj[:, 12:14, :])
                convolve(l)
                barrier()
                l2((0.125, 0.125, 1.0, 1.0))
                barrier()
                delta(l)
                barrier()
                gated_out(6, param(f"gdn_norm{l}"), proj[:, 20:22, :])
                barrier()
                project_out(mod[:, 0, 2, :])
                barrier()
                lower_panels()
                norm(x, h, mix)
                lower_panels()
                swiglu(mod[:, 0, 5, :])
                barrier()

            dve.wait_ge(sem["const_in"], 64)
            dve.wait_ge(sem["x_in"], 16)
            lower_bounds()
            conditions("start")
            for n in range(2):
                mod_column(PLANS["start"], n)
            coefficient(0, param("norm_mix0"), 1)
            barrier()
            for l in range(2):
                layer(l)

            def moe_layer(w):
                barrier()
                norm(x, h)
                barrier()
                experts(mod[:, w, 5, :])
                residual(mod[:, w, 5, :], "down", "down_x")
                barrier()

            norm(x, h)
            barrier()
            dve.wait_ge(*due("ctx_in", 32))
            norm(x_ctx, h_ctx)
            barrier()
            link(ts(stats[:, 240:241], param("gq"), 0.125, None, ALU.mult))
            barrier()
            rope([stats[:, 240:241]] * 4 + [param("gk")], table(even_t, "cos"), table(even_t, "sin"))
            barrier()
            head_norm_ctx()
            barrier()
            attention()
            barrier()
            conv_even()
            barrier()
            mlstm()
            barrier()
            project_out(mod[:, 0, 2, :])
            moe_layer(0)
            coefficient(0, param("norm11"), 1, 1)
            coefficient(1, param("norm21"), 4, 1)
            link(tt(coef[:, 3, :], mod[:, 1, 2, :], param("s_pool"), ALU.mult))
            barrier()
            lower_panels()
            norm(x, h, mix)
            lower_panels(3)
            barrier()
            dve.wait_ge(*due("pool_in", 16))
            pooling()
            residual(coef[:, 3, :], "down", "down_x")
            moe_layer(1)
            norm(x, h)


_INS = ["xT", "positions", "general", "first", "even", "pool", "params", "ada_w", "w_in", "w_out", "w_gate", "w_up",
        "w_down", "ctxT", "w_mod", "w_in_even", "w_out_even", "w_in_odd", "w_pool_grp", "w_exp_gate", "w_exp_up",
        "w_exp_down"]


def arrays(a):
    f = np.ascontiguousarray
    c = dict(zip(("general", "first", "even", "pool"), (packed(t)[0] for t in constants())))
    c["params"] = f(np.concatenate(list(parameters(a).values()), 1))
    c["xT"] = f(np.asarray(a["x"])[0].T)
    c["positions"] = f(np.asarray(a["positions"])[0])
    c["ctxT"] = f(np.asarray(a["ctx_2"])[0].T)
    for name in _INS:
        if name not in c:
            c[name] = f(np.asarray(a[name if name in a else name + "_2"]))
    return c


def kernel(**inputs):
    import concourse.bacc as _bacc
    from concourse.bass_utils import run_bass_kernel_spmd as _run

    nc = _bacc.Bacc("TRN2", target_bir_lowering=False, num_devices=1)
    given, args = {}, {}
    for name, v in arrays(inputs).items():
        given[f"in_{name}"] = v
        args[name] = nc.dram_tensor(f"in_{name}", v.shape, mybir.dt.from_np(v.dtype), kind="ExternalInput").ap()
    out = nc.dram_tensor("out", (D, T), F32, kind="ExternalOutput").ap()
    build(nc, args, out, packed(parameters(inputs))[1])
    r = _run(nc, [given], core_ids=[0])
    return np.ascontiguousarray(r.results[0]["out"].T)[None]
```
